# Optimizing a Trainium2 kernel written in Bass

```python
import math
import jax
import jax.numpy as jnp
from jax import lax
import numpy as np

D_MODEL = 1024
BATCH = 1
SEQ = 256
DEPTH = 2

POOL_WINDOWS = (2, 4, 8, 16)
POOL_GROUP_DIM = D_MODEL // 8
POOL_WIDTH = POOL_GROUP_DIM * len(POOL_WINDOWS)
ATTN_HEADS = 8
ATTN_HEAD_DIM = 64
ATTN_WIDTH = ATTN_HEADS * ATTN_HEAD_DIM
DILATED_BRANCHES = ((128, 1), (512, 4), (2048, 16))
ATTN_BLOCK = 128
EVEN_IN_WIDTH = POOL_WIDTH + 3 * ATTN_WIDTH
MIX_WIDTH = POOL_WIDTH + ATTN_WIDTH

SSM_EXPAND = 2
SSM_INNER = SSM_EXPAND * D_MODEL
SSM_HEAD_DIM = 64
SSM_HEADS = SSM_INNER // SSM_HEAD_DIM
SSM_GROUPS = 8
SSM_STATE = 128
SSM_CONV = 4
SSM_CHUNK = 128
SSM_CONV_DIM = SSM_INNER + 2 * SSM_GROUPS * SSM_STATE
SSM_IN_WIDTH = SSM_INNER + SSM_CONV_DIM + SSM_HEADS

PEER_HEADS = 8
PEER_N_KEYS = 128
PEER_N_EXPERTS = PEER_N_KEYS * PEER_N_KEYS
PEER_KEY_DIM = 256
PEER_HALF = PEER_KEY_DIM // 2
PEER_TOPK = 16
PEER_TOKEN_BLOCK = 128
PEER_V_SCALE = PEER_HEADS ** -0.5

N_EVEN = (DEPTH + 1) // 2
N_ODD = DEPTH // 2
EPS = 1e-6

kernel_name = 'hybrid_pool_dilattn_ssd_peer'

def rmsnorm(x, g):
    xf = x.astype(jnp.float32)
    y = xf * lax.rsqrt(jnp.mean(xf * xf, axis=-1, keepdims=True) + EPS)
    return (y * g.astype(jnp.float32)).astype(x.dtype)

def alibi_slopes(n):
    return 2.0 ** (-8.0 * jnp.arange(1, n + 1, dtype=jnp.float32) / n)

def causal_pool_mixer(a, pool_w, pool_scale):
    S = a.shape[1]
    af = a.astype(jnp.float32)
    csum = jnp.cumsum(af, axis=1)
    count = jnp.arange(1, S + 1, dtype=jnp.float32)[None, :, None]
    outs = []
    for i, w in enumerate(POOL_WINDOWS):
        sl = slice(i * POOL_GROUP_DIM, (i + 1) * POOL_GROUP_DIM)
        c = csum[..., sl]
        c_lag = jnp.pad(c, ((0, 0), (w, 0), (0, 0)))[:, :S]
        mean = (c - c_lag) / jnp.minimum(count, float(w))
        mixed = (mean - af[..., sl]).astype(a.dtype)
        outs.append(jnp.einsum('bsc,cd->bsd', mixed, pool_w[i]))
    return jnp.concatenate(outs, axis=-1) * pool_scale

def dilated_branch(q, k, v, window, dilation, slopes):
    Bsz, S, H, E = q.shape
    n_sub = window // dilation
    L = S // dilation
    nb = -(-L // ATTN_BLOCK)
    Lp = nb * ATTN_BLOCK

    def to_sub(t):
        t = t.reshape(Bsz, L, dilation, H, E).transpose(0, 2, 1, 3, 4)
        t = jnp.pad(t, ((0, 0), (0, 0), (0, Lp - L), (0, 0), (0, 0)))
        return t.reshape(Bsz, dilation, nb, ATTN_BLOCK, H, E)

    def with_prev(t):
        prev = jnp.pad(t, ((0, 0), (0, 0), (1, 0), (0, 0), (0, 0), (0, 0)))[:, :, :nb]
        return jnp.concatenate([prev, t], axis=3)

    qb = to_sub(q)
    kk = with_prev(to_sub(k))
    vv = with_prev(to_sub(v))
    s = jnp.einsum('brnqhe,brnkhe->brnhqk', qb, kk, preferred_element_type=jnp.float32)
    qi = jnp.arange(ATTN_BLOCK)[:, None]
    kj = jnp.arange(2 * ATTN_BLOCK)[None, :]
    dist = qi + ATTN_BLOCK - kj
    in_band = (dist >= 0) & (dist <= n_sub)
    has_prev = (jnp.arange(nb) > 0)[:, None, None] | (kj >= ATTN_BLOCK)[None]
    valid = in_band[None] & has_prev
    bias = -slopes[:, None, None] * (dist * dilation).astype(jnp.float32)[None]
    s = s * (ATTN_HEAD_DIM ** -0.5) + bias
    s = jnp.where(valid[:, None], s, -jnp.inf)
    m = jnp.max(s, axis=-1, keepdims=True)
    p = jnp.exp(s - m)
    l = jnp.sum(p, axis=-1, keepdims=True)
    o = jnp.einsum('brnhqk,brnkhe->brnhqe', p, vv.astype(jnp.float32)) / l
    lse = (m + jnp.log(l))[..., 0]
    o = o.transpose(0, 1, 2, 4, 3, 5).reshape(Bsz, dilation, Lp, H, E)[:, :, :L]
    o = o.transpose(0, 2, 1, 3, 4).reshape(Bsz, S, H, E)
    lse = lse.transpose(0, 1, 2, 4, 3).reshape(Bsz, dilation, Lp, H)[:, :, :L]
    lse = lse.transpose(0, 2, 1, 3).reshape(Bsz, S, H)
    return o, lse

def dilated_attention(qkv, q_gain, k_gain):
    Bsz, S, _ = qkv.shape
    q, k, v = jnp.split(qkv, 3, axis=-1)
    q = rmsnorm(q.reshape(Bsz, S, ATTN_HEADS, ATTN_HEAD_DIM), q_gain)
    k = rmsnorm(k.reshape(Bsz, S, ATTN_HEADS, ATTN_HEAD_DIM), k_gain)
    v = v.reshape(Bsz, S, ATTN_HEADS, ATTN_HEAD_DIM)
    slopes = alibi_slopes(ATTN_HEADS)
    outs, lses = [], []
    for window, dilation in DILATED_BRANCHES:
        o, lse = dilated_branch(q, k, v, window, dilation, slopes)
        outs.append(o)
        lses.append(lse)
    wts = jax.nn.softmax(jnp.stack(lses, axis=0), axis=0)
    o = wts[0][..., None] * outs[0] + wts[1][..., None] * outs[1] + wts[2][..., None] * outs[2]
    return o.reshape(Bsz, S, ATTN_WIDTH).astype(qkv.dtype)

def pool_attention_mixer(h, w_in, pool_w, pool_scale, q_gain, k_gain, w_out):
    proj = jnp.einsum('bsd,de->bse', h, w_in)
    a = causal_pool_mixer(proj[..., :POOL_WIDTH], pool_w, pool_scale).astype(h.dtype)
    o = dilated_attention(proj[..., POOL_WIDTH:], q_gain, k_gain)
    return jnp.einsum('bse,ed->bsd', jnp.concatenate([a, o], axis=-1), w_out)

def ssd_chunked_scan(x, dt, A, bm, cm):
    Bsz, S, H, P = x.shape
    G, N = bm.shape[2], bm.shape[3]
    R = H // G
    Q = SSM_CHUNK
    nc = S // Q
    xdt = (x.astype(jnp.float32) * dt[..., None]).reshape(Bsz, nc, Q, G, R, P)
    da = (dt * A).reshape(Bsz, nc, Q, G, R)
    bmc = bm.astype(jnp.float32).reshape(Bsz, nc, Q, G, N)
    cmc = cm.astype(jnp.float32).reshape(Bsz, nc, Q, G, N)
    xs = (jnp.moveaxis(xdt, 1, 0), jnp.moveaxis(da, 1, 0), jnp.moveaxis(bmc, 1, 0), jnp.moveaxis(cmc, 1, 0))
    causal = jnp.tril(jnp.ones((Q, Q), dtype=bool))[None, :, :, None, None]

    def step(state, inp):
        xdt_c, da_c, b_c, c_c = inp
        acum = jnp.cumsum(da_c, axis=1)
        seg = acum[:, :, None] - acum[:, None, :]
        decay = jnp.exp(jnp.where(causal, seg, -jnp.inf))
        cb = jnp.einsum('blgn,bsgn->blsg', c_c, b_c)
        y_diag = jnp.einsum('blsgr,bsgrp->blgrp', cb[..., None] * decay, xdt_c)
        y_off = jnp.einsum('blgn,bgrpn->blgrp', c_c, state) * jnp.exp(acum)[..., None]
        last = acum[:, -1]
        w_state = jnp.exp(last[:, None] - acum)
        new_state = state * jnp.exp(last)[..., None, None] + jnp.einsum(
            'bsgn,bsgrp->bgrpn', b_c, xdt_c * w_state[..., None])
        return new_state, y_diag + y_off

    init = jnp.zeros((Bsz, G, R, P, N), jnp.float32)
    _, ys = lax.scan(step, init, xs)
    return jnp.moveaxis(ys, 0, 1).reshape(Bsz, S, H, P)

def ssd_mixer(h, w_in, conv_w, conv_b, dt_bias, a_log, d_skip, gate_gain, w_out):
    Bsz, S, _ = h.shape
    proj = jnp.einsum('bsd,de->bse', h, w_in)
    z = proj[..., :SSM_INNER]
    xbc = proj[..., SSM_INNER:SSM_INNER + SSM_CONV_DIM]
    dt_raw = proj[..., SSM_INNER + SSM_CONV_DIM:]
    xbc = lax.conv_general_dilated(
        xbc, conv_w[:, None, :], window_strides=(1,), padding=[(SSM_CONV - 1, 0)],
        dimension_numbers=('NWC', 'WIO', 'NWC'), feature_group_count=SSM_CONV_DIM) + conv_b
    xbc = jax.nn.silu(xbc)
    xh = xbc[..., :SSM_INNER].reshape(Bsz, S, SSM_HEADS, SSM_HEAD_DIM)
    bm = xbc[..., SSM_INNER:SSM_INNER + SSM_GROUPS * SSM_STATE].reshape(Bsz, S, SSM_GROUPS, SSM_STATE)
    cm = xbc[..., SSM_INNER + SSM_GROUPS * SSM_STATE:].reshape(Bsz, S, SSM_GROUPS, SSM_STATE)
    dt = jax.nn.softplus(dt_raw.astype(jnp.float32) + dt_bias.astype(jnp.float32))
    A = -jnp.exp(a_log.astype(jnp.float32))
    y = ssd_chunked_scan(xh, dt, A, bm, cm)
    y = y + d_skip.astype(jnp.float32)[:, None] * xh.astype(jnp.float32)
    y = y.reshape(Bsz, S, SSM_INNER) * jax.nn.silu(z.astype(jnp.float32))
    y = rmsnorm(y.reshape(Bsz, S, SSM_GROUPS, SSM_INNER // SSM_GROUPS),
                gate_gain.reshape(SSM_GROUPS, SSM_INNER // SSM_GROUPS))
    y = y.reshape(Bsz, S, SSM_INNER).astype(h.dtype)
    return jnp.einsum('bse,ed->bsd', y, w_out)

def peer_ffn(h, w_q, sub_keys, expert_u, expert_v):
    Bsz, S, D = h.shape
    n = PEER_TOKEN_BLOCK
    hb = h.reshape((Bsz * S) // n, n, D)
    keys = sub_keys.astype(jnp.float32)

    def block(xb):
        q = jnp.einsum('nd,de->ne', xb, w_q).astype(jnp.float32).reshape(n, PEER_HEADS, 2, PEER_HALF)
        s = jnp.einsum('nhie,ike->nhik', q, keys)
        top_s, top_i = lax.top_k(s, PEER_TOPK)
        cand_s = (top_s[:, :, 0, :, None] + top_s[:, :, 1, None, :]).reshape(n, PEER_HEADS, PEER_TOPK * PEER_TOPK)
        cand_i = (top_i[:, :, 0, :, None] * PEER_N_KEYS + top_i[:, :, 1, None, :]).reshape(n, PEER_HEADS, PEER_TOPK * PEER_TOPK)
        best_s, best_pos = lax.top_k(cand_s, PEER_TOPK)
        idx = jnp.take_along_axis(cand_i, best_pos, axis=-1)
        gate = jax.nn.softmax(best_s, axis=-1)
        u = expert_u[idx]
        act = jax.nn.gelu(jnp.einsum('nhkd,nd->nhk', u, xb, preferred_element_type=jnp.float32), approximate=False)
        coef = (gate * act).astype(xb.dtype)
        return jnp.einsum('nhk,nhkd->nd', coef, expert_v[idx])

    return lax.map(block, hb).reshape(Bsz, S, D)

def setup_inputs(seed: int = 0) -> dict:
    key = jax.random.key(seed)
    ks = jax.random.split(key, 24)
    f32 = jnp.float32

    def nrm(k, shape, scale):
        return jax.random.normal(k, shape, f32) * scale

    x = nrm(ks[0], (BATCH, SEQ, D_MODEL), 1.0)
    attn_norm = 1.0 + nrm(ks[1], (DEPTH, D_MODEL), 0.1)
    ffn_norm = 1.0 + nrm(ks[2], (DEPTH, D_MODEL), 0.1)
    even_w_in = nrm(ks[3], (N_EVEN, D_MODEL, EVEN_IN_WIDTH), D_MODEL ** -0.5)
    pool_w = nrm(ks[4], (N_EVEN, len(POOL_WINDOWS), POOL_GROUP_DIM, POOL_GROUP_DIM), POOL_GROUP_DIM ** -0.5)
    pool_scale = 1.0 + nrm(ks[5], (N_EVEN, POOL_WIDTH), 0.1)
    q_gain = 1.0 + nrm(ks[6], (N_EVEN, ATTN_HEAD_DIM), 0.1)
    k_gain = 1.0 + nrm(ks[7], (N_EVEN, ATTN_HEAD_DIM), 0.1)
    even_w_out = nrm(ks[8], (N_EVEN, MIX_WIDTH, D_MODEL), MIX_WIDTH ** -0.5)
    ssm_w_in = nrm(ks[9], (N_ODD, D_MODEL, SSM_IN_WIDTH), D_MODEL ** -0.5)
    conv_w = nrm(ks[10], (N_ODD, SSM_CONV, SSM_CONV_DIM), SSM_CONV ** -0.5)
    conv_b = nrm(ks[11], (N_ODD, SSM_CONV_DIM), 0.02)
    dt0 = jnp.exp(jax.random.uniform(ks[12], (N_ODD, SSM_HEADS), f32, math.log(1e-3), math.log(1e-1)))
    dt_bias = dt0 + jnp.log(-jnp.expm1(-dt0))
    a_log = jnp.log(jax.random.uniform(ks[13], (N_ODD, SSM_HEADS), f32, 1.0, 16.0))
    d_skip = 1.0 + nrm(ks[14], (N_ODD, SSM_HEADS), 0.1)
    gate_gain = 1.0 + nrm(ks[15], (N_ODD, SSM_INNER), 0.1)
    ssm_w_out = nrm(ks[16], (N_ODD, SSM_INNER, D_MODEL), SSM_INNER ** -0.5)
    peer_w_q = nrm(ks[17], (DEPTH, D_MODEL, PEER_HEADS * PEER_KEY_DIM), D_MODEL ** -0.5)
    peer_sub_keys = nrm(ks[18], (DEPTH, 2, PEER_N_KEYS, PEER_HALF), PEER_HALF ** -0.5)
    peer_u = nrm(ks[19], (DEPTH, PEER_N_EXPERTS, D_MODEL), D_MODEL ** -0.5)
    peer_v = nrm(ks[20], (DEPTH, PEER_N_EXPERTS, D_MODEL), PEER_V_SCALE)
    return {'x': x, 'attn_norm': attn_norm, 'ffn_norm': ffn_norm, 'even_w_in': even_w_in,
            'pool_w': pool_w, 'pool_scale': pool_scale, 'q_gain': q_gain, 'k_gain': k_gain,
            'even_w_out': even_w_out, 'ssm_w_in': ssm_w_in, 'conv_w': conv_w, 'conv_b': conv_b,
            'dt_bias': dt_bias, 'a_log': a_log, 'd_skip': d_skip, 'gate_gain': gate_gain,
            'ssm_w_out': ssm_w_out, 'peer_w_q': peer_w_q, 'peer_sub_keys': peer_sub_keys,
            'peer_u': peer_u, 'peer_v': peer_v}

def reference(x, attn_norm, ffn_norm, even_w_in, pool_w, pool_scale, q_gain, k_gain, even_w_out,
              ssm_w_in, conv_w, conv_b, dt_bias, a_log, d_skip, gate_gain, ssm_w_out,
              peer_w_q, peer_sub_keys, peer_u, peer_v):
    h = x
    for layer in range(DEPTH):
        hn = rmsnorm(h, attn_norm[layer])
        i = layer // 2
        if layer % 2 == 0:
            mix = pool_attention_mixer(hn, even_w_in[i], pool_w[i], pool_scale[i], q_gain[i], k_gain[i], even_w_out[i])
        else:
            mix = ssd_mixer(hn, ssm_w_in[i], conv_w[i], conv_b[i], dt_bias[i], a_log[i], d_skip[i], gate_gain[i], ssm_w_out[i])
        h = h + mix.astype(h.dtype)
        ffn = peer_ffn(rmsnorm(h, ffn_norm[layer]), peer_w_q[layer], peer_sub_keys[layer], peer_u[layer], peer_v[layer])
        h = h + ffn.astype(h.dtype)
    return h


_drawn_inputs = setup_inputs


def setup_inputs(seed=0):
    import zlib

    import numpy as np

    out = dict(_drawn_inputs(seed))
    spreads = {}
    factors = {}
    for name, (base, spread) in spreads.items():
        noise = np.random.default_rng([zlib.crc32(name.encode()), seed]).standard_normal(out[name].shape)
        drawn = base * np.exp(spread * noise) if base else spread * noise
        out[name] = jnp.asarray(drawn.astype(out[name].dtype))
    for name, factor in factors.items():
        out[name] = (out[name] * factor).astype(out[name].dtype)
    return out
```

```python
import math
from contextlib import ExitStack

import numpy as np

import concourse.bass as bass
from concourse import mybir

P = 128
D = 1024
KD = D // P
SEQ = 256
NBLK = SEQ // P
DEPTH = 2
POOL_WINDOWS = (2, 4, 8, 16)
NWIN = len(POOL_WINDOWS)
HEADS, HD = 8, 64
AW = HEADS * HD
BRANCHES = ((128, 1), (512, 4), (2048, 16))
EPS = 1e-6
SH, SP_, SG, SN, TAPS = 32, 64, 8, 128, 4
SI = SH * SP_
HPG = SH // SG
GW = HPG * SP_
XBC = SI + 2 * SG * SN
XT = XBC // P
PH, NK, HALF, TOPK = 8, 128, 128, 16
M16 = 2 * PH
NEXP = NK * NK
SLOTS = PH * TOPK
CW = 512
CH = KD * CW
NEG = -1.0e30

RING = 8
GROUP = 4
BODY = 2 * RING
STEPS = SLOTS // BODY

NWB = 2
L0_CHUNKS = 4 + 2 + 4
L1_CHUNKS = 8 + 4 + 4 + 4

C_ID, C_TRI, C_STRI, C_IOTA = 0, P, 2 * P, 3 * P
C_END = C_IOTA + TOPK


def shape_constants():
    c = np.zeros((P, C_END), np.float32)
    row, col = np.arange(P)[:, None], np.arange(P)[None, :]
    c[:, C_ID:C_ID + P] = row == col
    c[:, C_TRI:C_TRI + P] = row <= col
    c[:, C_STRI:C_STRI + P] = row > col
    c[:, C_IOTA:] = np.arange(TOPK)
    bands = np.zeros((P, 3, NWIN, P), np.float32)
    for n, w in enumerate(POOL_WINDOWS):
        lag = col - row
        first = ((lag >= 0) & (lag < w)) / np.minimum(col + 1, w) - (lag == 0)
        later = ((lag >= 0) & (lag < w)) / w - (lag == 0)
        before = ((lag + P >= 0) & (lag + P < w)) / w
        for k, band in enumerate((first, later, before)):
            bands[:, k, n] = band
    return c, bands.reshape(P, -1)


def attention_bias():
    dist = np.arange(P)[:, None] + P - np.arange(2 * P)[None, :]
    count = np.zeros((P, 2 * P))
    for window, dilation in BRANCHES:
        count += (dist >= 0) & (dist <= window) & (dist % dilation == 0)
    logs = np.where(count > 0, np.log(np.maximum(count, 1)), NEG)
    slopes = 2.0 ** (-8.0 * np.arange(1, HEADS + 1) / HEADS)
    bias = -slopes[None, :, None] * dist[:, None, :] + logs[:, None, :]
    return np.ascontiguousarray(bias.reshape(P, HEADS * 2 * P).astype(np.float32))


def build_trunk(nc, io):
    f32, u32 = mybir.dt.float32, mybir.dt.uint32
    ALU = mybir.AluOpType
    ACT = mybir.ActivationFunctionType
    AX = mybir.AxisListType.X

    ctx = ExitStack()
    with ctx:
        def sb(name, cols, dt=f32):
            return ctx.enter_context(nc.sbuf_tensor(name, [P, cols], dt))[:, :]

        def bank(name):
            return ctx.enter_context(nc.psum_tensor(name, [P, CW], f32))[:, :]

        sems = {}

        def sem(name):
            if name not in sems:
                sems[name] = ctx.enter_context(nc.semaphore(name))
            return sems[name]

        h = sb("h", NBLK * D).rearrange("p (b d) -> p b d", b=NBLK)
        hn = sb("hn", NBLK * D).rearrange("p (b d) -> p b d", b=NBLK)
        hnT = sb("hnT", KD * SEQ).rearrange("p (k t) -> p k t", k=KD)
        gains = sb("gains", 2 * D).rearrange("p (n d) -> p n d", d=D)
        wbuf = sb("wbuf", NWB * CH).rearrange("p (n k c) -> p n k c", n=NWB, k=KD)
        ring = sb("ring", RING * 2 * D).rearrange("p (r d) -> p r d", r=RING)
        cst = sb("cst", C_END)
        keysT = sb("keysT", DEPTH * 2 * NK).rearrange("p (l i k) -> p l i k", l=DEPTH, i=2)
        rowc = sb("rowc", 2 * HD + 3 * SH)
        colc = sb("colc", NWIN + XT * TAPS + XT + 16)
        dtw = sb("dtw", KD * SH).rearrange("p (k c) -> p k c", k=KD)
        diag = sb("diag", 2 * GROUP * P).rearrange("p (n c) -> p n c", c=P)
        dots = sb("dots", BODY)
        acts = sb("acts", BODY)
        coefs = sb("coefs", BODY)
        idx_now = sb("idx_now", BODY, u32)
        idx = sb("idx", NBLK * SLOTS, u32)
        gate = sb("gate", NBLK * SLOTS)
        stat = sb("stat", 128)
        zrow = sb("zrow", P)
        eA = sb("eA", SH)

        ident = cst[:, C_ID:C_ID + P]
        tri = cst[:, C_TRI:C_TRI + P]
        stri = cst[:, C_STRI:C_STRI + P]
        iota16 = cst[:, C_IOTA:C_IOTA + 16]

        qk_gain = rowc[:, 0:2 * HD].rearrange("p (i e) -> p i e", i=2)
        dt_bias, a_log, d_skip = (rowc[:, 2 * HD + n * SH:2 * HD + (n + 1) * SH] for n in range(3))
        pool_scale = colc[:, 0:NWIN]
        taps = colc[:, NWIN:NWIN + XT * TAPS].rearrange("p (t j) -> p t j", j=TAPS)
        conv_b = colc[:, NWIN + XT * TAPS:NWIN + XT * TAPS + XT]
        gate_gain = colc[:, NWIN + XT * TAPS + XT:]

        SCRATCH = 16512
        scratch = sb("scratch", SCRATCH)

        class Carve:
            def __init__(self, start=0):
                self.at = start

            def __call__(self, size, pattern=None, **dims):
                part = scratch[:, self.at:self.at + size]
                self.at += size
                assert self.at <= SCRATCH, self.at
                return part.rearrange(pattern, **dims) if pattern else part

        cut = Carve()
        bias_t = cut(HEADS * 2 * P, "p (h k) -> p h k", h=HEADS)
        pool_in = cut(NBLK * AW, "p (b c) -> p b c", b=NBLK)
        qk = cut(NBLK * 2 * AW, "p (b i c) -> p b i c", b=NBLK, i=2)
        qk_sq = cut(2 * AW)
        bands = cut(3 * NWIN * P, "p (k n c) -> p k n c", k=3, n=NWIN)
        v_rows = cut(NBLK * AW, "p (b c) -> p b c", b=NBLK)
        qkT = cut(2 * 4 * SEQ, "p (i n t) -> p i n t", i=2, n=4)
        probs = cut(3 * 2 * P, "p (n k) -> p n k", n=3)
        probsT = cut(2 * 2 * P, "p (n j q) -> p n j q", n=2, j=2)
        pool_w = cut(NWIN * P, "p (n c) -> p n c", c=P)
        mixedT = cut(NWIN * P, "p (n c) -> p n c", c=P)
        mixT = cut(8 * SEQ, "p (k t) -> p k t", k=8)

        cut = Carve()
        conv_in = cut(2 * 4 * (P + TAPS - 1), "p (n j t) -> p n j t", n=2, j=4)
        xT = cut(2 * CW, "p (n c) -> p n c", n=2)
        bcT = cut(2 * SG * P, "p (g t) -> p g t", g=2 * SG)
        x_rows = cut(SI)
        b_rows = cut(SG * SN)
        xdt = cut(SI)
        y = cut(SI)
        decay = cut(2 * CW, "p (n r l) -> p n r l", n=2, r=HPG)
        cb = cut(SG * P, "p (g l) -> p g l", g=SG)
        y_tmp = cut(GW)
        dtv = cut(8 * SH, "p (n c) -> p n c", n=8)
        yT = bcT
        state = cut(SG * GW, "p (g c) -> p g c", g=SG)
        carry = cut(XT * (TAPS - 1), "p (t c) -> p t c", t=XT)
        kept_from = cut.at - SG * GW - XT * (TAPS - 1)

        cut = Carve()
        qT = cut(NBLK * M16 * P, "p (b m t) -> p b m t", b=NBLK, m=M16)
        scores = cut(M16 * NK, "p (m k) -> p m k", m=M16)
        cand = cut(PH * TOPK * TOPK, "p (h c) -> p h c", h=PH)
        onehot = cut(PH * TOPK * TOPK)
        top_s = cut(M16 * TOPK)
        top_i = cut(M16 * TOPK).bitcast(u32)
        top_if = cut(M16 * TOPK)
        best = cut(SLOTS)
        best_pos = cut(SLOTS).bitcast(u32)
        pos_hi = cut(SLOTS).bitcast(u32)
        pos_lo = cut(SLOTS).bitcast(u32)
        pos_f = cut(2 * SLOTS, "p (i s) -> p i s", i=2)
        picked = cut(2 * SLOTS, "p (i s) -> p i s", i=2)
        expd = cut(SLOTS)
        assert cut.at <= kept_from, (cut.at, kept_from)

        acc = [bank("acc0"), bank("acc1")]
        act_banks = [bank(f"act_bank{n}") for n in range(3)]
        dve_banks = [bank(f"dve_bank{n}") for n in range(3)]

        def gain_rows(layer):
            return io["gains"][layer:layer + 1].to_broadcast([P, 2, D])

        block = ctx.enter_context(nc.Block())

        class Lane:

            def __init__(self, eng, own):
                self.eng, self.own, self.count, self.seen = eng, own, {}, {}

            def __call__(self, instruction, name=None):
                name = name or self.own
                self.count[name] = self.count.get(name, 0) + 1
                instruction.then_inc(sem(name), 1)
                self.eng.wait_ge(sem(name), self.count[name])

            def tell(self, name):
                self.eng.sem_inc(sem(name), 1)

            def need(self, name):
                self.seen[name] = self.seen.get(name, 0) + 1
                self.eng.wait_ge(sem(name), self.seen[name])

        class Emptier:

            def __init__(self, eng, kind, banks):
                self.eng, self.kind, self.banks, self.n = eng, kind, banks, 0

            def take(self):
                self.eng.wait_ge(sem(self.kind + "_full"), self.n + 1)
                self.n += 1
                return self.banks[(self.n - 1) % 3]

        @block.sync
        def _(sp):
            sp.dma_start(h, io["x"].rearrange("(b p) d -> p b d", p=P)).then_inc(sem("x_loaded"), 16)
            sp.dma_start(gains, gain_rows(0)).then_inc(sem("gains_loaded"), 16)
            sp.dma_start(cst, io["consts"]).then_inc(sem("consts_loaded"), 16)

            def chunk(slot, t, at):
                sp.wait_ge(sem("chunks_free"), t + 1)
                sp.dma_start(wbuf[:, slot].rearrange("p k c -> p (k c)"),
                             io["weights"][at].rearrange("n p c -> p (n c)")).then_inc(sem(f"chunk_in{slot}"), 16)

            def layer_chunks(first, count, back):
                with sp.Fori(first // NWB, (first + count) // NWB) as pair:
                    for slot in range(NWB):
                        chunk(slot, pair * NWB + slot, bass.ds(pair * NWB + (slot - back), 1))

            layer_chunks(0, L0_CHUNKS, 0)
            layer_chunks(L0_CHUNKS, L1_CHUNKS, 0)
            layer_chunks(L0_CHUNKS + L1_CHUNKS, L1_CHUNKS, L1_CHUNKS)
            for b in range(NBLK):
                sp.wait_ge(sem("out_ready"), b + 1)
                sp.dma_start(io["out"][b * P:(b + 1) * P, :], h[:, b]).then_inc(sem("stored"), 16)
            sp.wait_ge(sem("stored"), 16 * NBLK)

        @block.gpsimd
        def _(pool):
            pool.memset(zrow, 0.0).then_inc(sem("zero_row"), 1)
            pool.dma_start(colc, io["cols"]).then_inc(sem("cols_loaded"), 16)
            pool.dma_start(rowc, io["rows"].to_broadcast([P, 2 * HD + 3 * SH])).then_inc(sem("rows_loaded"), 16)
            pool.dma_start(bias_t, io["bias"].rearrange("p (h k) -> p h k", h=HEADS)).then_inc(sem("bias_loaded"), 16)
            pool.dma_start(bands, io["bands"].rearrange("p (k n c) -> p k n c", k=3, n=NWIN)).then_inc(sem("pool_w_loaded"), 16)
            pool.dma_start(pool_w, io["pool_w"].rearrange("n c d -> c n d")).then_inc(sem("pool_w_loaded"), 16)
            pool.dma_start(keysT, io["keysT"].rearrange("l i e k -> e l i k")).then_inc(sem("keys_loaded"), 16)
            pool.dma_start(dtw, io["dt_w"].rearrange("(k p) c -> p k c", p=P)).then_inc(sem("dtw_loaded"), 16)

            def gather_step(phase, g):
                layer = phase // NBLK
                for j in range(2):
                    for s in range(RING):
                        if s % GROUP == 0:
                            q = j * 2 + s // GROUP
                            pool.wait_ge(sem("groups_free"), g * 4 + (q + 1))
                        if s == 0:
                            pool.wait_ge(sem("idx_ready"), phase + 1)
                            pool.tensor_copy(idx_now[:, j * RING:(j + 1) * RING],
                                             idx[:, bass.ds(g * BODY + (j * RING - layer * NBLK * SLOTS), RING)]
                                             ).then_inc(sem("idx_staged"), 1)
                            pool.wait_ge(sem("idx_staged"), g * 2 + (j + 1))
                        if s % GROUP == 0:
                            pool.sem_inc(sem("group_opened"), 1)
                        pool.indirect_dma_start(
                            ring[:, s], None, io[f"experts{layer}"],
                            bass.IndirectOffsetOnAxis(idx_now[:, j * RING + s:j * RING + s + 1], 0),
                        ).then_inc(sem(f"rows_in{s}"), 16)

            for phase in range(DEPTH * NBLK):
                pool.wait_ge(sem("idx_ready"), phase + 1)
                with pool.Fori(phase * STEPS, (phase + 1) * STEPS) as g:
                    gather_step(phase, g)

        @block.tensor
        def _(pe):
            lane = Lane(pe, "pe_own")
            jobs = {"act": 0, "dve": 0}
            chunks = [0]

            def fill(kind):
                n = jobs[kind]
                if n >= 3:
                    pe.wait_ge(sem(kind + "_emptied"), n - 2)
                jobs[kind] = n + 1
                return (act_banks if kind == "act" else dve_banks)[n % 3], n + 1

            def emptied(kind, number):
                pe.wait_ge(sem(kind + "_emptied"), number)

            def next_chunk():
                n = chunks[0]
                chunks[0] += 1
                pe.wait_ge(sem(f"chunk_in{n % NWB}"), 16 * (n // NWB + 1))
                return wbuf[:, n % NWB]

            def chunk_used(kind):
                pe.wait_ge(sem(kind + "_full"), jobs[kind])
                pe.sem_inc(sem("chunks_free"), 1)

            def project_rows(out, lhsT, w, first=True, last=True, cols=CW):
                for k in range(KD):
                    ins = pe.matmul(out[:, 0:cols], lhsT[:, k], w[:, k], start=first and k == 0,
                                    stop=last and k == KD - 1)
                return ins

            def transposes(src, n):
                out, number = fill("act")
                for j in range(n):
                    ins = pe.transpose(out[:, j * P:(j + 1) * P], src[:, j * P:(j + 1) * P], ident)
                ins.then_inc(sem("act_full"), 1)
                return number

            def norm_transposes(b):
                lane.need("hn_ready")
                transposes(hn[:, b, 0:4 * P], 4)
                emptied("act", transposes(hn[:, b, 4 * P:8 * P], 4))

            def mixer0():
                for b in range(NBLK):
                    norm_transposes(b)
                    yield
                numbers = {}
                for c, (what, kind) in enumerate((("pool", "act"), ("q", "dve"), ("k", "dve"), ("v", "act"))):
                    w = next_chunk()
                    for b in range(NBLK):
                        out, numbers[what, b] = fill(kind)
                        project_rows(out, hnT[:, :, b * P:(b + 1) * P], w).then_inc(sem(kind + "_full"), 1)
                    chunk_used(kind)
                for b in range(NBLK):
                    lane.need("qk_ready")
                    for i in range(2):
                        last_qkT = transposes(qk[:, b, i], 4)
                pe.wait_ge(sem("pool_w_loaded"), 32)
                for b in range(NBLK):
                    emptied("act", numbers["pool", b])
                    out, number = fill("act")
                    for n in range(NWIN):
                        cols = slice(n * P, (n + 1) * P)
                        ins = pe.matmul(out[:, cols], pool_in[:, b, cols], bands[:, min(b, 1), n],
                                        start=True, stop=b == 0)
                        if b:
                            ins = pe.matmul(out[:, cols], pool_in[:, b - 1, cols], bands[:, 2, n],
                                            start=False, stop=True)
                    ins.then_inc(sem("act_full"), 1)
                    emptied("act", number)
                    out, number = fill("dve")
                    for n in range(NWIN):
                        ins = pe.matmul(out[:, n * P:(n + 1) * P], pool_w[:, n], mixedT[:, n],
                                        start=True, stop=True)
                    ins.then_inc(sem("dve_full"), 1)
                emptied("act", last_qkT)

                def score(b, hd):
                    off = hd % 2 * HD
                    keys = (b + 1) * P
                    out, _ = fill("dve")
                    pe.matmul(out[:, 0:keys], qkT[off:off + HD, 0, hd // 2, b * P:(b + 1) * P],
                              qkT[off:off + HD, 1, hd // 2, 0:keys], start=True, stop=True
                              ).then_inc(sem("dve_full"), 1)

                pairs = [(b, hd) for b in range(NBLK) for hd in range(HEADS)]
                score(*pairs[0])
                score(*pairs[1])
                for n, (b, hd) in enumerate(pairs):
                    if n + 2 < len(pairs):
                        score(*pairs[n + 2])
                    lane.need("probs_ready")
                    out, _ = fill("act")
                    for j in range(b + 1):
                        ins = pe.transpose(out[:, j * P:(j + 1) * P], probs[:, n % 3, j * P:(j + 1) * P], ident)
                    ins.then_inc(sem("act_full"), 1)
                    if hd % 2:
                        emptied("act", jobs["act"])
                        out, number = fill("act")
                        for m in range(2):
                            head = hd - 1 + m
                            for j in range(b + 1):
                                ins = pe.matmul(out[m * HD:(m + 1) * HD, 0:P],
                                                v_rows[:, j, head * HD:(head + 1) * HD],
                                                probsT[:, m, j], start=j == 0, stop=j == b)
                        ins.then_inc(sem("act_full"), 1)
                        yield
                emptied("act", number)
                emptied("dve", jobs["dve"])
                for n in range(2):
                    w = next_chunk()
                    for b in range(NBLK):
                        out, _ = fill("dve")
                        project_rows(out, mixT[:, :, b * P:(b + 1) * P], w).then_inc(sem("dve_full"), 1)
                    chunk_used("dve")
                    yield

            def mixer1(b):
                tok = slice(b * P, (b + 1) * P)
                norm_transposes(b)
                yield
                pe.wait_ge(sem("dtw_loaded"), 16)
                out, _ = fill("dve")
                project_rows(out, hnT[:, :, tok], dtw, cols=SH).then_inc(sem("dve_full"), 1)

                def chunk_products():
                    w = next_chunk()
                    out, number = fill("act")
                    for j in range(4):
                        for k in range(KD):
                            ins = pe.matmul(out[:, j * P:(j + 1) * P], w[:, k, j * P:(j + 1) * P],
                                            hnT[:, k, tok], start=k == 0, stop=k == KD - 1)
                        if j < 3:
                            yield
                    ins.then_inc(sem("act_full"), 1)
                    chunk_used("act")
                    yield

                def chunk_transposes(c):
                    if c >= 6:
                        return
                    lane.need("conv_ready")
                    src = xT[:, c % 2] if c < 4 else bcT[:, (c - 4) * 4:(c - 3) * 4].rearrange("p g t -> p (g t)")
                    transposes(src, 4)

                for c in range(8):
                    yield from chunk_products()
                    if c == 0:
                        lane.need("da_ready")
                        out, _ = fill("dve")
                        pe.matmul(out[:, 0:SH], tri, dtv[:, 1], start=True, stop=True)
                        pe.matmul(out[:, SH:2 * SH], stri, dtv[:, 1], start=True, stop=True
                                  ).then_inc(sem("dve_full"), 1)
                    if c >= 1:
                        chunk_transposes(c - 1)
                    yield
                lane.need("bc_ready")
                for half in range(2):
                    out, _ = fill("dve")
                    for j in range(4):
                        g = half * 4 + j
                        ins = pe.matmul(out[:, j * P:(j + 1) * P], bcT[:, g], bcT[:, SG + g], start=True, stop=True)
                    ins.then_inc(sem("dve_full"), 1)
                yield

                def decays(g):
                    out, _ = fill("dve")
                    for r in range(HPG):
                        head = g * HPG + r
                        ins = pe.matmul(out[:, r * P:(r + 1) * P], dtv[:, 1, head:head + 1].to_broadcast([P, P]),
                                        tri, start=True, stop=True)
                    ins.then_inc(sem("dve_full"), 1)

                def group_out(g):
                    lane.need("weights_ready")
                    out, _ = fill("dve")
                    for r in range(HPG):
                        head = g * HPG + r
                        ins = pe.matmul(out[:, r * SP_:(r + 1) * SP_], decay[:, g % 2, r],
                                        xdt[:, head * SP_:(head + 1) * SP_], start=True, stop=True)
                    if b:
                        ins = pe.matmul(out[:, GW:2 * GW], bcT[:, SG + g], state[:, g], start=True, stop=True)
                    ins.then_inc(sem("dve_full"), 1)

                if b + 1 < NBLK:
                    lane.need("xdtw_ready")
                    for half in range(4):
                        out, number = fill("act")
                        for j in range(2):
                            g = half * 2 + j
                            ins = pe.matmul(out[:, j * GW:(j + 1) * GW], b_rows[:, g * SN:(g + 1) * SN],
                                            y[:, g * GW:(g + 1) * GW], start=True, stop=True)
                        ins.then_inc(sem("act_full"), 1)
                        yield
                    pe.wait_ge(sem("act_full"), jobs["act"])
                    pe.sem_inc(sem("xdtw_taken"), 1)
                decays(0)
                for g in range(SG):
                    if g + 1 < SG:
                        decays(g + 1)
                    group_out(g)
                    yield
                for c in range(4):
                    w = next_chunk()
                    out, _ = fill("act")
                    project_rows(out, hnT[:, :, tok], w).then_inc(sem("act_full"), 1)
                    chunk_used("act")
                    yield
                lane.need("y_ready")
                for c in range(4):
                    out, number = fill("dve")
                    for j in range(4):
                        k = c * 4 + j
                        ins = pe.transpose(out[:, j * P:(j + 1) * P], y[:, k * P:(k + 1) * P], ident)
                    ins.then_inc(sem("dve_full"), 1)
                    yield
                emptied("dve", number)
                yTk = yT.rearrange("p (half k) t -> p half k t", half=2)
                for n in range(2):
                    out, _ = fill("dve")
                    for half in range(2):
                        w = next_chunk()
                        ins = project_rows(out, yTk[:, half], w, first=half == 0, last=half == 1)
                        if half:
                            ins.then_inc(sem("dve_full"), 1)
                            chunk_used("dve")
                        else:
                            lane(ins)
                            pe.sem_inc(sem("chunks_free"), 1)
                        yield

            def queries(layer, blocks):
                for b in blocks:
                    norm_transposes(b)
                pe.wait_ge(sem("keys_loaded"), 16)
                for c in range(4):
                    w = next_chunk()
                    for b in blocks:
                        out, _ = fill("act")
                        for j in range(4):
                            for k in range(KD):
                                ins = pe.matmul(out[:, j * P:(j + 1) * P], w[:, k, j * P:(j + 1) * P],
                                                hnT[:, k, b * P:(b + 1) * P], start=k == 0, stop=k == KD - 1)
                            if j < 3:
                                yield
                        ins.then_inc(sem("act_full"), 1)
                    chunk_used("act")
                    yield

            def key_scores(layer, b):
                emptied("act", jobs["act"])
                for c in range(4):
                    out, _ = fill("act")
                    for j in range(4):
                        m = c * 4 + j
                        ins = pe.matmul(out[:, j * NK:(j + 1) * NK], qT[:, b, m], keysT[:, layer, m % 2],
                                        start=True, stop=True)
                    ins.then_inc(sem("act_full"), 1)
                    yield

            def expert_step(phase, g):
                for q in range(4):
                    pe.wait_ge(sem("diag_ready"), g * 4 + (q + 1))
                    for s in range(GROUP):
                        slot = (q % 2) * GROUP + s
                        for n in range(2):
                            ins = pe.matmul(acc[n], diag[:, slot], ring[:, slot, D + n * CW:D + (n + 1) * CW],
                                            start=False, stop=False, skip_group_check=True)
                    ins.then_inc(sem("groups_free"), 1)

            def experts(phase):
                if phase:
                    pe.wait_ge(sem("acc_read"), phase)
                b = phase % NBLK
                for n in range(2):
                    pe.matmul(acc[n], zrow[0:1, :], hn[0:1, b, n * CW:(n + 1) * CW], start=True, stop=False,
                              skip_group_check=True)
                with pe.Fori(phase * STEPS, (phase + 1) * STEPS) as g:
                    expert_step(phase, g)
                for n in range(2):
                    ins = pe.matmul(acc[n], zrow[0:1, :], hn[0:1, b, n * CW:(n + 1) * CW], start=False, stop=True,
                                    skip_group_check=True)
                ins.then_inc(sem("acc_full"), 1)

            def run(steps):
                for _ in steps:
                    pass

            pe.sem_inc(sem("chunks_free"), NWB)
            pe.sem_inc(sem("groups_free"), 2)
            pe.wait_ge(sem("consts_loaded"), 16)
            pe.wait_ge(sem("zero_row"), 1)
            run(mixer0())
            run(queries(0, range(NBLK)))
            for b in range(NBLK):
                run(key_scores(0, b))
            for b in range(NBLK):
                experts(b)
            for b in range(NBLK):
                run(mixer1(b))
                run(queries(1, [b]))
                run(key_scores(1, b))
            for b in range(NBLK):
                experts(NBLK + b)

        @block.scalar
        def _(act):
            lane = Lane(act, "act_own")
            ring_in = Emptier(act, "act", act_banks)

            def f(out, in_, func, name=None, **more):
                lane(act.activation(out, in_, func, **more), name)

            def empty(out, func=ACT.Copy, pattern=None, cols=CW, **dims):
                src = ring_in.take()[:, 0:cols]
                f(out, src.rearrange(pattern, **dims) if pattern else src, func, "act_emptied")

            def inverse_root(n):
                lane.need("root_asked")
                f(stat[:, 16:16 + n], stat[:, 0:n], ACT.Ln)
                f(stat[:, 32:32 + n], stat[:, 16:16 + n], ACT.Exp, scale=-0.5)
                lane.tell("root_given")

            def norm(b):
                inverse_root(1)
                for n in range(2):
                    empty(hnT[:, 4 * n:4 * n + 4, b * P:(b + 1) * P], pattern="p (k t) -> p k t", k=4)

            def mixer0():
                act.wait_ge(sem("rows_loaded"), 16)
                f(eA, a_log, ACT.Exp)
                for b in range(NBLK):
                    norm(b)
                for b in range(NBLK):
                    empty(pool_in[:, b])
                for b in range(NBLK):
                    empty(v_rows[:, b])
                for b in range(NBLK):
                    inverse_root(2 * HEADS)
                    for i in range(2):
                        empty(qkT[:, i, :, b * P:(b + 1) * P], pattern="p (n t) -> p n t", n=4)
                for b in range(NBLK):
                    empty(mixedT, pattern="p (n c) -> p n c", n=NWIN)

                def exp_scores(n, b):
                    lane.need("scores_biased")
                    keys = (b + 1) * P
                    f(probs[:, n % 3, 0:keys], probs[:, n % 3, 0:keys], ACT.Exp,
                      bias=stat[:, 64 + n % 3:65 + n % 3], accum_out=stat[:, 68 + n % 3:69 + n % 3])
                    lane.tell("scores_exp")

                pairs = [(b, hd) for b in range(NBLK) for hd in range(HEADS)]
                exp_scores(0, 0)
                for n, (b, hd) in enumerate(pairs):
                    if n + 1 < len(pairs):
                        exp_scores(n + 1, pairs[n + 1][0])
                    empty(probsT[:, n % 2, 0:b + 1], pattern="p (j q) -> p j q", cols=(b + 1) * P, j=b + 1)
                    lane.tell("probs_taken")
                    if hd % 2:
                        empty(mixT[:, NWIN + hd // 2, b * P:(b + 1) * P], cols=P)
                    yield

            def mixer1(b):
                norm(b)
                yield
                lane.need("dt_abs")
                f(dtv[:, 6], dtv[:, 2], ACT.Exp, scale=-1.0)
                f(dtv[:, 6], dtv[:, 6], ACT.Ln, bias=1.0)
                lane.tell("dt_log")
                yield
                for c in range(9):
                    if c < 8:
                        if c >= 2:
                            lane.need("conv_done")
                        empty(conv_in[:, c % 2, :, TAPS - 1:], pattern="p (j t) -> p j t", j=4)
                        lane.tell("conv_loaded")
                    else:
                        lane.need("conv_done")
                    if c >= 1:
                        d = c - 1
                        act.wait_ge(sem("conv_done"), 8 * b + d + 1)
                        if d < 4:
                            f(xT[:, d % 2], xT[:, d % 2], ACT.Silu)
                        else:
                            f(bcT[:, (d - 4) * 4:(d - 3) * 4].rearrange("p g t -> p (g t)"), xT[:, d % 2], ACT.Silu)
                        if d < 6:
                            lane.tell("conv_ready")
                            empty(x_rows[:, d * CW:(d + 1) * CW] if d < 4 else b_rows[:, (d - 4) * CW:(d - 3) * CW])
                            lane.tell("conv_rows")
                        if d == 0:
                            lane.need("sums_ready")
                            f(dtv[:, 5:7].rearrange("p n c -> p (n c)"), dtv[:, 3:5].rearrange("p n c -> p (n c)"), ACT.Exp)
                            lane.tell("decay_factors")
                    yield
                lane.need("conv_done")
                lane.tell("bc_ready")
                if b + 1 < NBLK:
                    for half in range(4):
                        empty(state[:, 2 * half:2 * half + 2], pattern="p (g c) -> p g c", g=2)
                        yield
                for g in range(SG):
                    lane.need("decay_args")
                    f(decay[:, g % 2], decay[:, g % 2], ACT.Exp)
                    lane.tell("decay_exp")
                    yield
                for c in range(4):
                    if c >= 2:
                        act.wait_ge(sem("z_used"), 4 * b + c - 1)
                    empty(xT[:, c % 2], ACT.Silu)
                    lane.tell("z_ready")
                    yield
                inverse_root(SG)
                yield

            def queries(layer, blocks):
                for b in blocks:
                    norm(b)
                if layer == 0:
                    act.dma_start(gains, gain_rows(1)).then_inc(sem("gains_loaded"), 16)
                for c in range(4):
                    for b in blocks:
                        empty(qT[:, b, 4 * c:4 * c + 4], pattern="p (m t) -> p m t", m=4)
                        yield

            def key_scores(layer, b):
                if layer == 0 and b:
                    lane.need("scores_used")
                for c in range(4):
                    empty(scores[:, 4 * c:4 * c + 4], pattern="p (m k) -> p m k", m=4)
                    lane.tell("scores_ready")
                    yield

            def softmax_exp():
                lane.need("best_ready")
                f(expd, expd, ACT.Exp)
                lane.tell("best_exp")
                yield

            def expert_step(phase, g):
                for q in range(4):
                    cols = slice(q * GROUP, (q + 1) * GROUP)
                    act.wait_ge(sem("dot_done"), g * BODY + (q + 1) * GROUP)
                    act.activation(acts[:, cols], dots[:, cols], ACT.Gelu).then_inc(sem("gelu_done"), 1)
                    act.wait_ge(sem("coef_done"), g * 4 + (q + 1))
                    act.wait_ge(sem("groups_free"), g * 4 + (q + 1))
                    for s in range(GROUP):
                        ins = act.activation(diag[:, (q % 2) * GROUP + s], ident, ACT.Copy,
                                             scale=coefs[:, q * GROUP + s:q * GROUP + s + 1])
                    ins.then_inc(sem("diag_ready"), 1)

            def experts(phase):
                with act.Fori(phase * STEPS, (phase + 1) * STEPS) as g:
                    expert_step(phase, g)

            def run(steps):
                for _ in steps:
                    pass

            act.wait_ge(sem("consts_loaded"), 16)
            run(mixer0())
            run(queries(0, range(NBLK)))
            for b in range(NBLK):
                run(key_scores(0, b))
                run(softmax_exp())
            for b in range(NBLK):
                experts(b)
            for b in range(NBLK):
                run(mixer1(b))
                run(queries(1, [b]))
                run(key_scores(1, b))
                run(softmax_exp())
            for b in range(NBLK):
                experts(NBLK + b)

        @block.vector
        def _(dve):
            lane = Lane(dve, "dve_own")
            ring_in = Emptier(dve, "dve", dve_banks)

            def tt(out, in0, in1, op=ALU.mult, name=None):
                lane(dve.tensor_tensor(out, in0, in1, op), name)

            def ts(out, in0, s1, s2, op0, op1=None, name=None):
                more = () if op1 is None else (op1,)
                lane(dve.tensor_scalar(out, in0, s1, s2, op0, *more), name)

            def stt(out, in0, scalar, in1, op0, op1, name=None):
                lane(dve.scalar_tensor_tensor(out, in0, scalar, in1, op0, op1), name)

            def add_to_stream(b, n, src, name):
                part = h[:, b, n * CW:(n + 1) * CW]
                tt(part, part, src, ALU.add, name)

            def inverse_root(n):
                v, r, t = stat[:, 0:n], stat[:, 32:32 + n], stat[:, 48:48 + n]
                lane.tell("root_asked")
                lane.need("root_given")
                tt(t, r, r)
                tt(t, t, v)
                ts(t, t, -0.5, 1.5, ALU.mult, ALU.add)
                tt(r, r, t)

            def norm(layer, which, b):
                dve.wait_ge(sem("gains_loaded"), 16 * (layer + 1))
                lane(dve.tensor_tensor_reduce(out=hn[:, b], in0=h[:, b], in1=h[:, b], scale=1.0, scalar=0.0,
                                              op0=ALU.mult, op1=ALU.add, accum_out=stat[:, 0:1]))
                ts(stat[:, 0:1], stat[:, 0:1], 1.0 / D, EPS, ALU.mult, ALU.add)
                inverse_root(1)
                stt(hn[:, b], h[:, b], stat[:, 32:33], gains[:, which], ALU.mult, ALU.mult)
                lane.tell("hn_ready")

            def mixer0():
                dve.wait_ge(sem("x_loaded"), 16)
                for b in range(NBLK):
                    norm(0, 0, b)
                for i in range(2):
                    for b in range(NBLK):
                        lane(dve.tensor_copy(qk[:, b, i], ring_in.take()), "dve_emptied")
                dve.wait_ge(sem("rows_loaded"), 16)
                for b in range(NBLK):
                    flat = qk[:, b].rearrange("p i c -> p (i c)")
                    heads = flat.rearrange("p (m e) -> p m e", e=HD)
                    tt(qk_sq, flat, flat)
                    lane(dve.reduce_sum(stat[:, 0:16], qk_sq.rearrange("p (m e) -> p m e", e=HD), AX))
                    ts(stat[:, 0:16], stat[:, 0:16], 1.0 / HD, EPS, ALU.mult, ALU.add)
                    inverse_root(2 * HEADS)
                    tt(heads, heads, stat[:, 32:48].unsqueeze(2).to_broadcast([P, 2 * HEADS, HD]))
                    for i in range(2):
                        part = qk[:, b, i].rearrange("p (m e) -> p m e", e=HD)
                        tt(part, part, qk_gain[:, i:i + 1].to_broadcast([P, HEADS, HD]))
                    lane.tell("qk_ready")
                dve.wait_ge(sem("cols_loaded"), 16)
                for b in range(NBLK):
                    tt(mixT[:, 0:NWIN, b * P:(b + 1) * P], ring_in.take().rearrange("p (n t) -> p n t", n=NWIN),
                       pool_scale.unsqueeze(2).to_broadcast([P, NWIN, P]), name="dve_emptied")
                dve.wait_ge(sem("bias_loaded"), 16)

                def bias_scores(n, b, hd):
                    if n >= 3:
                        lane.need("probs_taken")
                    keys = (b + 1) * P
                    part = probs[:, n % 3, 0:keys]
                    stt(part, ring_in.take()[:, 0:keys], HD ** -0.5, bias_t[:, hd, 2 * P - keys:],
                        ALU.mult, ALU.add, "dve_emptied")
                    top = stat[:, 64 + n % 3:65 + n % 3]
                    lane(dve.reduce_max(top, part, AX))
                    ts(top, top, -1.0, None, ALU.mult)
                    lane.tell("scores_biased")

                pairs = [(b, hd) for b in range(NBLK) for hd in range(HEADS)]
                bias_scores(0, *pairs[0])
                for n, (b, hd) in enumerate(pairs):
                    if n + 1 < len(pairs):
                        bias_scores(n + 1, *pairs[n + 1])
                    lane.need("scores_exp")
                    total = stat[:, 68 + n % 3:69 + n % 3]
                    part = probs[:, n % 3, 0:(b + 1) * P]
                    lane(dve.reciprocal(total, total))
                    ts(part, part, total, None, ALU.mult)
                    lane.tell("probs_ready")
                    yield
                for n in range(2):
                    for b in range(NBLK):
                        add_to_stream(b, n, ring_in.take(), "dve_emptied")
                        yield

            def mixer1(b):
                norm(1, 0, b)
                yield
                tt(dtv[:, 0], ring_in.take()[:, 0:SH], dt_bias, ALU.add, "dve_emptied")
                stt(dtv[:, 2], dtv[:, 0], -1.0, dtv[:, 0], ALU.mult, ALU.max)
                lane.tell("dt_abs")
                lane.need("dt_log")
                stt(dtv[:, 0], dtv[:, 0], 0.0, dtv[:, 6], ALU.max, ALU.add)
                stt(dtv[:, 1], dtv[:, 0], -1.0, eA, ALU.mult, ALU.mult)
                lane.tell("da_ready")
                yield
                for c in range(8):
                    if c >= 2:
                        lane.need("conv_rows")
                    lane.need("conv_loaded")
                    tiles = conv_in[:, c % 2]
                    tails = carry[:, 4 * c:4 * c + 4]
                    if b:
                        lane(dve.tensor_copy(tiles[:, :, 0:TAPS - 1], tails))
                    else:
                        lane(dve.memset(tiles[:, :, 0:TAPS - 1], 0.0))
                        lane(dve.tensor_copy(tails, tiles[:, :, P:]))
                    for j in range(4):
                        t = 4 * c + j
                        out = xT[:, c % 2, j * P:(j + 1) * P]
                        ts(out, tiles[:, j, 0:P], taps[:, t, 0:1], conv_b[:, t:t + 1], ALU.mult, ALU.add)
                        for tap in range(1, TAPS):
                            stt(out, tiles[:, j, tap:tap + P], taps[:, t, tap:tap + 1], out, ALU.mult, ALU.add)
                        if j == 1:
                            yield
                    lane.tell("conv_done")
                    if c == 0:
                        lane(dve.tensor_copy(dtv[:, 3:5].rearrange("p n c -> p (n c)"), ring_in.take()[:, 0:2 * SH]),
                             "dve_emptied")
                        lane.tell("sums_ready")
                    yield
                by_head = "p (h e) -> p h e"
                step = dtv[:, 0].unsqueeze(2).to_broadcast([P, SH, SP_])
                tt(xdt.rearrange(by_head, h=SH), x_rows.rearrange(by_head, h=SH), step)
                yield
                lane.need("decay_factors")
                if b + 1 < NBLK:
                    tt(y.rearrange(by_head, h=SH), xdt.rearrange(by_head, h=SH),
                       dtv[:, 6].unsqueeze(2).to_broadcast([P, SH, SP_]))
                    lane.tell("xdtw_ready")
                    yield
                for half in range(2):
                    tt(cb[:, 4 * half:4 * half + 4], ring_in.take().rearrange("p (g l) -> p g l", g=4),
                       tri.unsqueeze(1).to_broadcast([P, 4, P]), name="dve_emptied")
                if b + 1 < NBLK:
                    lane.need("xdtw_taken")
                tt(y.rearrange(by_head, h=SH), x_rows.rearrange(by_head, h=SH),
                   d_skip.unsqueeze(2).to_broadcast([P, SH, SP_]))
                yield

                def decay_args(g):
                    out = ring_in.take()
                    for r in range(HPG):
                        head = g * HPG + r
                        ts(decay[:, g % 2, r], out[:, r * P:(r + 1) * P], dtv[:, 3, head:head + 1], 0.0,
                           ALU.subtract, ALU.min, "dve_emptied" if r == HPG - 1 else None)
                    lane.tell("decay_args")

                def group_out(g):
                    out = ring_in.take()
                    part = y[:, g * GW:(g + 1) * GW]
                    if b:
                        tt(y_tmp.rearrange(by_head, h=HPG), out[:, GW:2 * GW].rearrange(by_head, h=HPG),
                           dtv[:, 5, g * HPG:(g + 1) * HPG].unsqueeze(2).to_broadcast([P, HPG, SP_]))
                        tt(part, part, y_tmp, ALU.add)
                    tt(part, part, out[:, 0:GW], ALU.add, "dve_emptied")

                decay_args(0)
                for g in range(SG):
                    if g:
                        group_out(g - 1)
                    if g + 1 < SG:
                        decay_args(g + 1)
                    lane.need("decay_exp")
                    tt(decay[:, g % 2], decay[:, g % 2], cb[:, g:g + 1].to_broadcast([P, HPG, P]))
                    lane.tell("weights_ready")
                    yield
                group_out(SG - 1)
                for c in range(4):
                    lane.need("z_ready")
                    part = y[:, c * CW:(c + 1) * CW]
                    tt(part, part, xT[:, c % 2])
                    lane.tell("z_used")
                    yield
                grouped = y.rearrange("p (g c) -> p g c", g=SG)
                tt(x_rows, y, y)
                lane(dve.reduce_sum(stat[:, 0:SG], x_rows.rearrange("p (g c) -> p g c", g=SG), AX))
                ts(stat[:, 0:SG], stat[:, 0:SG], 1.0 / GW, EPS, ALU.mult, ALU.add)
                inverse_root(SG)
                yield
                tt(grouped, grouped, stat[:, 32:32 + SG].unsqueeze(2).to_broadcast([P, SG, GW]))
                lane.tell("y_ready")
                yield
                for c in range(4):
                    tt(yT[:, 4 * c:4 * c + 4], ring_in.take().rearrange("p (k t) -> p k t", k=4),
                       gate_gain[:, 4 * c:4 * c + 4].unsqueeze(2).to_broadcast([P, 4, P]), name="dve_emptied")
                yield
                for n in range(2):
                    add_to_stream(b, n, ring_in.take(), "dve_emptied")
                    yield

            def top16(src, values, places):
                lane(dve.max(values[:, 0:8], src))
                lane(dve.max_index(places[:, 0:8], values[:, 0:8], src))
                lane(dve.match_replace(src, values[:, 0:8], src, NEG))
                lane(dve.max(values[:, 8:16], src))
                lane(dve.max_index(places[:, 8:16], values[:, 8:16], src))

            def routing(layer, b):
                for c in range(4):
                    lane.need("scores_ready")
                    for j in range(4):
                        m = 4 * c + j
                        cols = slice(m * TOPK, (m + 1) * TOPK)
                        top16(scores[:, m], top_s[:, cols], top_i[:, cols])
                        yield
                if layer == 0 and b == 0:
                    lane.tell("scores_used")
                halves = top_s.rearrange("p (h i a) -> p i h a", i=2, a=TOPK)
                square = [P, PH, TOPK, TOPK]
                grid = cand.rearrange("p h (a b) -> p h a b", a=TOPK)
                for hd in range(PH):
                    a = halves[:, 0, hd].unsqueeze(2).to_broadcast([P, TOPK, TOPK])
                    c = halves[:, 1, hd].unsqueeze(1).to_broadcast([P, TOPK, TOPK])
                    tt(grid[:, hd], a, c, ALU.add)
                    cols = slice(hd * TOPK, (hd + 1) * TOPK)
                    top16(cand[:, hd], best[:, cols], best_pos[:, cols])
                    yield
                ts(pos_hi, best_pos, 4, None, ALU.logical_shift_right)
                ts(pos_lo, best_pos, 15, None, ALU.bitwise_and)
                lane(dve.tensor_copy(pos_f[:, 0], pos_hi))
                lane(dve.tensor_copy(pos_f[:, 1], pos_lo))
                lane(dve.tensor_copy(top_if, top_i))
                yield
                keys = top_if.rearrange("p (h i a) -> p i h a", i=2, a=TOPK)
                hot = onehot.rearrange("p (h s a) -> p h s a", h=PH, s=TOPK)
                hot_flat = onehot.rearrange("p (n a) -> p n a", a=TOPK)
                for i in range(2):
                    tt(hot_flat, pos_f[:, i].unsqueeze(2).to_broadcast([P, SLOTS, TOPK]),
                       iota16.unsqueeze(1).to_broadcast([P, SLOTS, TOPK]), ALU.is_equal)
                    yield
                    tt(hot, hot, keys[:, i].unsqueeze(2).to_broadcast(square))
                    yield
                    lane(dve.reduce_sum(picked[:, i], hot_flat, AX))
                    yield
                stt(pos_f[:, 0], picked[:, 0], float(NK), picked[:, 1], ALU.mult, ALU.add)
                lane(dve.tensor_copy(idx[:, b * SLOTS:(b + 1) * SLOTS], pos_f[:, 0]))
                lane.tell("idx_ready")
                by_head = best.rearrange("p (h s) -> p h s", h=PH)
                exps = expd.rearrange("p (h s) -> p h s", h=PH)
                tt(exps, by_head, by_head[:, :, 0:1].to_broadcast([P, PH, TOPK]), ALU.subtract)
                lane.tell("best_ready")
                lane.need("best_exp")
                lane(dve.reduce_sum(stat[:, 72:72 + PH], exps, AX))
                lane(dve.reciprocal(stat[:, 72:72 + PH], stat[:, 72:72 + PH]))
                tt(gate[:, b * SLOTS:(b + 1) * SLOTS].rearrange("p (h s) -> p h s", h=PH), exps,
                   stat[:, 72:72 + PH].unsqueeze(2).to_broadcast([P, PH, TOPK]))
                yield

            def expert_step(phase, g):
                layer, b = divmod(phase, NBLK)
                for q in range(4):
                    for s in range(GROUP):
                        slot = (q % 2) * GROUP + s
                        col = q * GROUP + s
                        dve.wait_ge(sem(f"rows_in{slot}"), g * 32 + 16 * (q // 2 + 1))
                        dve.tensor_tensor_reduce(out=ring[:, slot, 0:D], in0=ring[:, slot, 0:D], in1=hn[:, b],
                                                 scale=1.0, scalar=0.0, op0=ALU.mult, op1=ALU.add,
                                                 accum_out=dots[:, col:col + 1]).then_inc(sem("dot_done"), 1)
                        dve.wait_ge(sem("dot_done"), g * BODY + (col + 1))
                    dve.wait_ge(sem("gelu_done"), g * 4 + (q + 1))
                    cols = slice(q * GROUP, (q + 1) * GROUP)
                    dve.tensor_tensor(coefs[:, cols], acts[:, cols],
                                      gate[:, bass.ds(g * BODY + (q * GROUP - layer * NBLK * SLOTS), GROUP)],
                                      ALU.mult).then_inc(sem("coef_done"), 1)

            def experts(phase):
                with dve.Fori(phase * STEPS, (phase + 1) * STEPS) as g:
                    expert_step(phase, g)
                dve.wait_ge(sem("acc_full"), phase + 1)
                for n in range(2):
                    add_to_stream(phase % NBLK, n, acc[n], None)
                lane.tell("acc_read")
                if phase // NBLK == DEPTH - 1:
                    lane.tell("out_ready")

            def run(steps):
                for _ in steps:
                    pass

            dve.wait_ge(sem("consts_loaded"), 16)
            run(mixer0())
            for b in range(NBLK):
                norm(0, 1, b)
            for b in range(NBLK):
                run(routing(0, b))
            for b in range(NBLK):
                experts(b)
            for b in range(NBLK):
                run(mixer1(b))
                norm(1, 1, b)
                run(routing(1, b))
            for b in range(NBLK):
                experts(NBLK + b)


def chunked(w):
    k, n = w.shape
    w = w.reshape(k // D, KD, P, n // CW, CW)
    return w.transpose(3, 0, 2, 1, 4).reshape(-1, P, CH)


def tiles_last(v):
    return v.reshape(-1, P).T


def kernel(**inputs):
    import concourse.bacc as bacc
    from concourse.bass_utils import run_bass_kernel_spmd

    a = {k: np.asarray(v) for k, v in inputs.items()}
    w_in = a["ssm_w_in"][0]
    pool_first = a["even_w_in"][0]
    consts, bands = shape_constants()
    weights = [chunked(pool_first), chunked(a["even_w_out"][0]), chunked(a["peer_w_q"][0]),
               chunked(w_in[:, SI:SI + XBC]), chunked(w_in[:, 0:SI]), chunked(a["ssm_w_out"][0]),
               chunked(a["peer_w_q"][1])]
    conv_w = a["conv_w"][0].reshape(TAPS, XT, P).transpose(2, 1, 0).reshape(P, XT * TAPS)
    arrays = {
        "x": a["x"].reshape(SEQ, D),
        "gains": np.stack([a["attn_norm"], a["ffn_norm"]], axis=1),
        "weights": np.concatenate(weights, axis=0),
        "dt_w": w_in[:, SI + XBC:],
        "rows": np.concatenate([a["q_gain"][0], a["k_gain"][0], a["dt_bias"][0], a["a_log"][0],
                                a["d_skip"][0]])[None, :],
        "cols": np.concatenate([tiles_last(a["pool_scale"][0]), conv_w, tiles_last(a["conv_b"][0]),
                                tiles_last(a["gate_gain"][0])], axis=1),
        "pool_w": a["pool_w"][0],
        "keysT": a["peer_sub_keys"].transpose(0, 1, 3, 2),
        "experts0": np.concatenate([a["peer_u"][0], a["peer_v"][0]], axis=1),
        "experts1": np.concatenate([a["peer_u"][1], a["peer_v"][1]], axis=1),
        "consts": consts, "bands": bands, "bias": attention_bias(),
    }
    arrays = {"in_" + k: np.ascontiguousarray(v) for k, v in arrays.items()}
    nc = bacc.Bacc("TRN2", target_bir_lowering=False, num_devices=1)
    io = {k[3:]: nc.dram_tensor(k, v.shape, mybir.dt.from_np(v.dtype), kind="ExternalInput").ap()
          for k, v in arrays.items()}
    io["out"] = nc.dram_tensor("out", (SEQ, D), mybir.dt.float32, kind="ExternalOutput").ap()
    build_trunk(nc, io)
    r = run_bass_kernel_spmd(nc, [arrays], core_ids=[0])
    return r.results[0]["out"].reshape(1, SEQ, D)
```

```python
import math
from contextlib import ExitStack

import numpy as np

import concourse.bass as bass
from concourse import mybir

P = 128
D = 1024
KD = D // P
SEQ = 256
NBLK = SEQ // P
DEPTH = 2
POOL_WINDOWS = (2, 4, 8, 16)
NWIN = len(POOL_WINDOWS)
HEADS, HD = 8, 64
AW = HEADS * HD
BRANCHES = ((128, 1), (512, 4), (2048, 16))
EPS = 1e-6
SH, SP_, SG, SN, TAPS = 32, 64, 8, 128, 4
SI = SH * SP_
HPG = SH // SG
GW = HPG * SP_
XBC = SI + 2 * SG * SN
XT = XBC // P
PH, NK, HALF, TOPK = 8, 128, 128, 16
M16 = 2 * PH
NEXP = NK * NK
SLOTS = PH * TOPK
CW = 512
CH = KD * CW
NEG = -1.0e30

RING = 8
GROUP = 4
BODY = 2 * RING
STEPS = SLOTS // BODY

NWB = 2
L0_CHUNKS = 4 + 2 + 4
L1_CHUNKS = 8 + 4 + 4 + 4

UNROLLED = {0: 6, 1: 8, 2: 8, 3: 0}
SIDE_TICKS = {0: 96, 1: 152, 2: 152}

T_NORM = 3
T_IN0 = T_NORM
T_ATT = T_IN0 + 16 + 3
T_OUT0 = T_ATT + 2 * HEADS + 1
T_END0 = T_OUT0 + 8 + 1
T_IN1 = T_NORM + 3
T_CB = T_IN1 + 32 + 3
T_SCAN = T_CB + 7
T_Z = T_SCAN + 2 * SG
T_YT = T_Z + 16 + 3
T_OUT1 = T_YT + 3
T_END1 = T_OUT1 + 16 + 1
T_Q = T_NORM
T_KEYS = T_Q + 16 + 1
T_TOP = T_KEYS + 2

C_ID, C_TRI, C_STRI, C_IOTA = 0, P, 2 * P, 3 * P
C_END = C_IOTA + TOPK


def shape_constants():
    c = np.zeros((P, C_END), np.float32)
    row, col = np.arange(P)[:, None], np.arange(P)[None, :]
    c[:, C_ID:C_ID + P] = row == col
    c[:, C_TRI:C_TRI + P] = row <= col
    c[:, C_STRI:C_STRI + P] = row > col
    c[:, C_IOTA:] = np.arange(TOPK)
    bands = np.zeros((P, 3, NWIN, P), np.float32)
    for n, w in enumerate(POOL_WINDOWS):
        lag = col - row
        first = ((lag >= 0) & (lag < w)) / np.minimum(col + 1, w) - (lag == 0)
        later = ((lag >= 0) & (lag < w)) / w - (lag == 0)
        before = ((lag + P >= 0) & (lag + P < w)) / w
        for k, band in enumerate((first, later, before)):
            bands[:, k, n] = band
    return c, bands.reshape(P, -1)


def attention_bias():
    dist = np.arange(P)[:, None] + P - np.arange(2 * P)[None, :]
    count = np.zeros((P, 2 * P))
    for window, dilation in BRANCHES:
        count += (dist >= 0) & (dist <= window) & (dist % dilation == 0)
    logs = np.where(count > 0, np.log(np.maximum(count, 1)), NEG)
    slopes = 2.0 ** (-8.0 * np.arange(1, HEADS + 1) / HEADS)
    bias = -slopes[None, :, None] * dist[:, None, :] + logs[:, None, :]
    return np.ascontiguousarray(bias.reshape(P, HEADS * 2 * P).astype(np.float32))


def build_trunk(nc, io):
    f32, u32 = mybir.dt.float32, mybir.dt.uint32
    ALU = mybir.AluOpType
    ACT = mybir.ActivationFunctionType
    AX = mybir.AxisListType.X

    ctx = ExitStack()
    with ctx:
        def sb(name, cols, dt=f32):
            return ctx.enter_context(nc.sbuf_tensor(name, [P, cols], dt))[:, :]

        def bank(name):
            return ctx.enter_context(nc.psum_tensor(name, [P, CW], f32))[:, :]

        sems = {}

        def sem(name):
            if name not in sems:
                sems[name] = ctx.enter_context(nc.semaphore(name))
            return sems[name]

        h = sb("h", NBLK * D).rearrange("p (b d) -> p b d", b=NBLK)
        hn = sb("hn", NBLK * D).rearrange("p (b d) -> p b d", b=NBLK)
        hnT = sb("hnT", KD * P).rearrange("p (k t) -> p k t", k=KD)
        gains = sb("gains", 2 * D).rearrange("p (n d) -> p n d", d=D)
        wbuf = sb("wbuf", NWB * CH).rearrange("p (n k c) -> p n k c", n=NWB, k=KD)
        ring = sb("ring", RING * 2 * D).rearrange("p (r d) -> p r d", r=RING)
        cst = sb("cst", C_END)
        keysT = sb("keysT", DEPTH * 2 * NK).rearrange("p (l i k) -> p l i k", l=DEPTH, i=2)
        rowc = sb("rowc", 2 * HD + 3 * SH)
        colc = sb("colc", NWIN + XT * TAPS + XT + 16)
        dtw = sb("dtw", KD * SH).rearrange("p (k c) -> p k c", k=KD)
        diag = sb("diag", 2 * GROUP * P).rearrange("p (n c) -> p n c", c=P)
        dots = sb("dots", BODY)
        acts = sb("acts", BODY)
        coefs = sb("coefs", BODY)
        idx_now = sb("idx_now", BODY, u32)
        idx = sb("idx", NBLK * SLOTS, u32)
        gate = sb("gate", NBLK * SLOTS)
        stat = sb("stat", 128)
        zrow = sb("zrow", P)
        eA = sb("eA", SH)

        ident = cst[:, C_ID:C_ID + P]
        tri = cst[:, C_TRI:C_TRI + P]
        stri = cst[:, C_STRI:C_STRI + P]
        iota16 = cst[:, C_IOTA:C_IOTA + 16]

        qk_gain = rowc[:, 0:2 * HD].rearrange("p (i e) -> p i e", i=2)
        dt_bias, a_log, d_skip = (rowc[:, 2 * HD + n * SH:2 * HD + (n + 1) * SH] for n in range(3))
        pool_scale = colc[:, 0:NWIN]
        taps = colc[:, NWIN:NWIN + XT * TAPS].rearrange("p (t j) -> p t j", j=TAPS)
        conv_b = colc[:, NWIN + XT * TAPS:NWIN + XT * TAPS + XT]
        gate_gain = colc[:, NWIN + XT * TAPS + XT:]

        SCRATCH = 17408
        ROUTING = 10240
        scratch = sb("scratch", SCRATCH)

        class Carve:
            def __init__(self, start=0, end=SCRATCH):
                self.at, self.end = start, end

            def __call__(self, size, pattern=None, **dims):
                part = scratch[:, self.at:self.at + size]
                self.at += size
                assert self.at <= self.end, self.at
                return part.rearrange(pattern, **dims) if pattern else part

        cut = Carve(end=ROUTING)
        qk = cut(2 * AW, "p (i c) -> p i c", i=2)
        qk_sq = cut(2 * AW)
        qT_att = cut(4 * P, "p (n t) -> p n t", n=4)
        probs = cut(3 * 2 * P, "p (n k) -> p n k", n=3)
        probsT = cut(2 * 2 * P, "p (n j q) -> p n j q", n=2, j=2)
        mixedT = cut(NWIN * P, "p (n c) -> p n c", c=P)
        mixT = cut(8 * P, "p (k t) -> p k t", k=8)
        cut = Carve(ROUTING)
        bias_t = cut(HEADS * 2 * P, "p (h k) -> p h k", h=HEADS)
        bands = cut(3 * NWIN * P, "p (k n c) -> p k n c", k=3, n=NWIN)
        pool_w = cut(NWIN * P, "p (n c) -> p n c", c=P)
        pool_in = cut(NBLK * AW, "p (b c) -> p b c", b=NBLK)
        v_rows = cut(NBLK * AW, "p (b c) -> p b c", b=NBLK)
        kT = cut(4 * SEQ, "p (n t) -> p n t", n=4)

        cut = Carve()
        conv_in = cut(2 * 4 * (P + TAPS - 1), "p (n j t) -> p n j t", n=2, j=4)
        xT = cut(2 * CW, "p (n c) -> p n c", n=2)
        bcT = cut(2 * SG * P, "p (g t) -> p g t", g=2 * SG)
        x_rows = cut(SI)
        b_rows = cut(SG * SN)
        xdt = cut(SI)
        y_tmp = cut(GW)
        dtv = cut(8 * SH, "p (n c) -> p n c", n=8)
        decay = cut(2 * CW, "p (n r l) -> p n r l", n=2, r=HPG)
        yT = bcT
        assert cut.at >= ROUTING
        state = cut(SG * GW, "p (g c) -> p g c", g=SG)
        carry = cut(XT * (TAPS - 1), "p (t c) -> p t c", t=XT)
        y = cut(SI)
        cb = cut(SG * P, "p (g l) -> p g l", g=SG)

        cut = Carve(end=ROUTING)
        qT = cut(M16 * P, "p (m t) -> p m t", m=M16)
        scores = cut(M16 * NK, "p (m k) -> p m k", m=M16)
        cand = cut(PH * TOPK * TOPK, "p (h c) -> p h c", h=PH)
        onehot = cut(PH * TOPK * TOPK)
        top_s = cut(M16 * TOPK)
        top_i = cut(M16 * TOPK).bitcast(u32)
        top_if = cut(M16 * TOPK)
        best = cut(SLOTS)
        best_pos = cut(SLOTS).bitcast(u32)
        pos_hi = cut(SLOTS).bitcast(u32)
        pos_lo = cut(SLOTS).bitcast(u32)
        pos_f = cut(2 * SLOTS, "p (i s) -> p i s", i=2)
        picked = cut(2 * SLOTS, "p (i s) -> p i s", i=2)
        expd = cut(SLOTS)

        acc = [bank("acc0"), bank("acc1")]
        act_banks = [bank(f"act_bank{n}") for n in range(3)]
        dve_banks = [bank(f"dve_bank{n}") for n in range(3)]

        def gain_rows(layer):
            return io["gains"][layer:layer + 1].to_broadcast([P, 2, D])

        block = ctx.enter_context(nc.Block())

        class Lane:

            def __init__(self, eng, own):
                self.eng, self.own, self.count, self.seen = eng, own, {}, {}

            def __call__(self, instruction, name=None):
                name = name or self.own
                self.count[name] = self.count.get(name, 0) + 1
                instruction.then_inc(sem(name), 1)
                self.eng.wait_ge(sem(name), self.count[name])

            def tell(self, name):
                self.eng.sem_inc(sem(name), 1)

            def need(self, name):
                self.seen[name] = self.seen.get(name, 0) + 1
                self.eng.wait_ge(sem(name), self.seen[name])

        class Emptier:

            def __init__(self, eng, kind, banks):
                self.eng, self.kind, self.banks, self.n = eng, kind, banks, 0

            def take(self):
                self.eng.wait_ge(sem(self.kind + "_full"), self.n + 1)
                self.n += 1
                return self.banks[(self.n - 1) % 3]

        class Side:

            def __init__(self, steps):
                self.steps, self.tick = steps, 0

            def upto(self, tick):
                while self.tick <= tick:
                    self.tick = next(self.steps, math.inf)

            def finish(self):
                for _ in self.steps:
                    pass
                self.tick = math.inf

        def pace(phase, n):
            return n * SIDE_TICKS[phase] / (UNROLLED[phase] * BODY)

        @block.sync
        def _(sp):
            sp.dma_start(h, io["x"].rearrange("(b p) d -> p b d", p=P)).then_inc(sem("x_loaded"), 16)
            sp.dma_start(gains, gain_rows(0)).then_inc(sem("gains_loaded"), 16)
            sp.dma_start(cst, io["consts"]).then_inc(sem("consts_loaded"), 16)

            def chunk(slot, t, at):
                sp.wait_ge(sem("chunks_free"), t + 1)
                sp.dma_start(wbuf[:, slot].rearrange("p k c -> p (k c)"),
                             io["weights"][at].rearrange("n p c -> p (n c)")).then_inc(sem(f"chunk_in{slot}"), 16)

            def layer_chunks(first, count, back):
                with sp.Fori(first // NWB, (first + count) // NWB) as pair:
                    for slot in range(NWB):
                        chunk(slot, pair * NWB + slot, bass.ds(pair * NWB + (slot - back), 1))

            layer_chunks(0, L0_CHUNKS, 0)
            layer_chunks(L0_CHUNKS, L0_CHUNKS, L0_CHUNKS)
            layer_chunks(2 * L0_CHUNKS, L1_CHUNKS, L0_CHUNKS)
            layer_chunks(2 * L0_CHUNKS + L1_CHUNKS, L1_CHUNKS, L0_CHUNKS + L1_CHUNKS)
            for b in range(NBLK):
                sp.wait_ge(sem("out_ready"), b + 1)
                sp.dma_start(io["out"][b * P:(b + 1) * P, :], h[:, b]).then_inc(sem("stored"), 16)
            sp.wait_ge(sem("stored"), 16 * NBLK)

        @block.gpsimd
        def _(pool):
            pool.memset(zrow, 0.0).then_inc(sem("zero_row"), 1)
            pool.dma_start(colc, io["cols"]).then_inc(sem("cols_loaded"), 16)
            pool.dma_start(rowc, io["rows"].to_broadcast([P, 2 * HD + 3 * SH])).then_inc(sem("rows_loaded"), 16)
            pool.dma_start(bias_t, io["bias"].rearrange("p (h k) -> p h k", h=HEADS)).then_inc(sem("bias_loaded"), 16)
            pool.dma_start(bands, io["bands"].rearrange("p (k n c) -> p k n c", k=3, n=NWIN)).then_inc(sem("pool_w_loaded"), 16)
            pool.dma_start(pool_w, io["pool_w"].rearrange("n c d -> c n d")).then_inc(sem("pool_w_loaded"), 16)
            pool.dma_start(keysT, io["keysT"].rearrange("l i e k -> e l i k")).then_inc(sem("keys_loaded"), 16)
            pool.dma_start(dtw, io["dt_w"].rearrange("(k p) c -> p k c", p=P)).then_inc(sem("dtw_loaded"), 16)

            def gather_step(phase, g):
                layer = phase // NBLK
                for j in range(2):
                    for s in range(RING):
                        pool.wait_ge(sem("slots_free"), g * BODY + (j * RING + s + 1))
                        pool.sem_inc(sem("slot_opened"), 1)
                        if s == 0:
                            pool.tensor_copy(idx_now[:, j * RING:(j + 1) * RING],
                                             idx[:, bass.ds(g * BODY + (j * RING - layer * NBLK * SLOTS), RING)]
                                             ).then_inc(sem("idx_staged"), 1)
                            pool.wait_ge(sem("idx_staged"), g * 2 + (j + 1))
                            pool.sem_inc(sem("slot_opened"), 1)
                        pool.indirect_dma_start(
                            ring[:, s], None, io[f"experts{layer}"],
                            bass.IndirectOffsetOnAxis(idx_now[:, j * RING + s:j * RING + s + 1], 0),
                        ).then_inc(sem(f"rows_in{s}"), 16)

            for phase in range(DEPTH * NBLK):
                pool.wait_ge(sem("idx_ready"), phase + 1)
                with pool.Fori(phase * STEPS, (phase + 1) * STEPS) as g:
                    gather_step(phase, g)

        @block.tensor
        def _(pe):
            lane = Lane(pe, "pe_own")
            jobs = {"act": 0, "dve": 0}
            chunks = [0]

            def fill(kind):
                n = jobs[kind]
                if n >= 3:
                    pe.wait_ge(sem(kind + "_emptied"), n - 2)
                jobs[kind] = n + 1
                return (act_banks if kind == "act" else dve_banks)[n % 3]

            def emptied(kind, number=None):
                pe.wait_ge(sem(kind + "_emptied"), number or jobs[kind])

            def next_chunk():
                n = chunks[0]
                chunks[0] += 1
                pe.wait_ge(sem(f"chunk_in{n % NWB}"), 16 * (n // NWB + 1))
                return wbuf[:, n % NWB]

            def chunk_used(kind):
                pe.wait_ge(sem(kind + "_full"), jobs[kind])
                pe.sem_inc(sem("chunks_free"), 1)

            def row_products(out, lhsT, w, first=True, last=True, cols=CW, tick=None):
                for k in range(KD):
                    ins = pe.matmul(out[:, 0:cols], lhsT[:, k], w[:, k], start=first and k == 0,
                                    stop=last and k == KD - 1)
                    if tick is not None and k % 2 and k < KD - 1:
                        yield tick + k // 2 + 1
                return ins

            def column_products(out, w, tick):
                for j in range(4):
                    for k in range(KD):
                        ins = pe.matmul(out[:, j * P:(j + 1) * P], w[:, k, j * P:(j + 1) * P], hnT[:, k],
                                        start=k == 0, stop=k == KD - 1)
                    if j < 3:
                        yield tick + j + 1
                return ins

            def transposes(src, n, kind="act"):
                out = fill(kind)
                for j in range(n):
                    ins = pe.transpose(out[:, j * P:(j + 1) * P], src[:, j * P:(j + 1) * P], ident)
                ins.then_inc(sem(kind + "_full"), 1)

            def norm_transposes(b):
                lane.need("hn_ready")
                transposes(hn[:, b, 0:4 * P], 4)
                transposes(hn[:, b, 4 * P:8 * P], 4)

            def mixer0(b):
                yield 1
                norm_transposes(b)
                emptied("act")
                for c, kind in enumerate(("act", "dve", "dve", "act")):
                    yield T_IN0 + 4 * c
                    w = next_chunk()
                    out = fill(kind)
                    ins = yield from row_products(out, hnT, w, tick=T_IN0 + 4 * c)
                    ins.then_inc(sem(kind + "_full"), 1)
                    chunk_used(kind)
                    if c == 0:
                        pooled = jobs["act"]
                yield T_IN0 + 16
                lane.need("qk_ready")
                for i in range(2):
                    transposes(qk[:, i], 4)
                qk_in = jobs["act"]
                yield T_IN0 + 17
                pe.wait_ge(sem("pool_w_loaded"), 32)
                emptied("act", pooled)
                out = fill("act")
                for n in range(NWIN):
                    cols = slice(n * P, (n + 1) * P)
                    ins = pe.matmul(out[:, cols], pool_in[:, b, cols], bands[:, min(b, 1), n],
                                    start=True, stop=b == 0)
                    if b:
                        ins = pe.matmul(out[:, cols], pool_in[:, b - 1, cols], bands[:, 2, n],
                                        start=False, stop=True)
                ins.then_inc(sem("act_full"), 1)
                yield T_IN0 + 18
                emptied("act")
                out = fill("dve")
                for n in range(NWIN):
                    ins = pe.matmul(out[:, n * P:(n + 1) * P], pool_w[:, n], mixedT[:, n],
                                    start=True, stop=True)
                ins.then_inc(sem("dve_full"), 1)
                yield T_ATT - 1
                emptied("act", qk_in)

                def score(hd):
                    off = hd % 2 * HD
                    keys = (b + 1) * P
                    out = fill("dve")
                    pe.matmul(out[:, 0:keys], qT_att[off:off + HD, hd // 2], kT[off:off + HD, hd // 2, 0:keys],
                              start=True, stop=True).then_inc(sem("dve_full"), 1)

                score(0)
                score(1)
                for hd in range(HEADS):
                    yield T_ATT + 2 * hd
                    if hd + 2 < HEADS:
                        score(hd + 2)
                    yield T_ATT + 2 * hd + 1
                    lane.need("probs_ready")
                    transposes(probs[:, hd % 3], b + 1)
                    if hd % 2:
                        emptied("act")
                        out = fill("act")
                        for m in range(2):
                            head = hd - 1 + m
                            for j in range(b + 1):
                                ins = pe.matmul(out[m * HD:(m + 1) * HD, 0:P],
                                                v_rows[:, j, head * HD:(head + 1) * HD],
                                                probsT[:, m, j], start=j == 0, stop=j == b)
                        ins.then_inc(sem("act_full"), 1)
                for n in range(2):
                    yield T_OUT0 + 4 * n
                    if n == 0:
                        emptied("act")
                        emptied("dve")
                    w = next_chunk()
                    out = fill("dve")
                    ins = yield from row_products(out, mixT, w, tick=T_OUT0 + 4 * n)
                    ins.then_inc(sem("dve_full"), 1)
                    chunk_used("dve")

            def mixer1(b):
                yield 1
                norm_transposes(b)
                emptied("act")
                yield T_NORM
                pe.wait_ge(sem("dtw_loaded"), 16)
                out = fill("dve")
                ins = yield from row_products(out, hnT, dtw, cols=SH)
                ins.then_inc(sem("dve_full"), 1)
                for c in range(8):
                    at = T_IN1 + 4 * c
                    yield at
                    if c == 1:
                        lane.need("da_ready")
                        out = fill("dve")
                        pe.matmul(out[:, 0:SH], tri, dtv[:, 1], start=True, stop=True)
                        pe.matmul(out[:, SH:2 * SH], stri, dtv[:, 1], start=True, stop=True
                                  ).then_inc(sem("dve_full"), 1)
                    if c >= 2:
                        lane.need("conv_ready")
                        d = c - 2
                        transposes(xT[:, d % 2] if d < 4 else
                                   bcT[:, (d - 4) * 4:(d - 3) * 4].rearrange("p g t -> p (g t)"), 4)
                    w = next_chunk()
                    out = fill("act")
                    ins = yield from column_products(out, w, at)
                    ins.then_inc(sem("act_full"), 1)
                    chunk_used("act")
                yield T_CB
                lane.need("bc_ready")
                for half in range(2):
                    out = fill("dve")
                    for j in range(4):
                        g = half * 4 + j
                        ins = pe.matmul(out[:, j * P:(j + 1) * P], bcT[:, g], bcT[:, SG + g], start=True, stop=True)
                    ins.then_inc(sem("dve_full"), 1)
                    yield T_CB + 1
                if b + 1 < NBLK:
                    lane.need("xdtw_ready")
                    for half in range(4):
                        yield T_CB + 2 + half
                        out = fill("act")
                        for j in range(2):
                            g = half * 2 + j
                            ins = pe.matmul(out[:, j * GW:(j + 1) * GW], b_rows[:, g * SN:(g + 1) * SN],
                                            y[:, g * GW:(g + 1) * GW], start=True, stop=True)
                        ins.then_inc(sem("act_full"), 1)
                    pe.wait_ge(sem("act_full"), jobs["act"])
                    pe.sem_inc(sem("xdtw_taken"), 1)

                def decays(g):
                    out = fill("dve")
                    for r in range(HPG):
                        head = g * HPG + r
                        ins = pe.matmul(out[:, r * P:(r + 1) * P], dtv[:, 1, head:head + 1].to_broadcast([P, P]),
                                        tri, start=True, stop=True)
                    ins.then_inc(sem("dve_full"), 1)

                def group_out(g):
                    lane.need("weights_ready")
                    out = fill("dve")
                    for r in range(HPG):
                        head = g * HPG + r
                        ins = pe.matmul(out[:, r * SP_:(r + 1) * SP_], decay[:, g % 2, r],
                                        xdt[:, head * SP_:(head + 1) * SP_], start=True, stop=True)
                    if b:
                        ins = pe.matmul(out[:, GW:2 * GW], bcT[:, SG + g], state[:, g], start=True, stop=True)
                    ins.then_inc(sem("dve_full"), 1)

                yield T_SCAN - 1
                decays(0)
                for g in range(SG):
                    yield T_SCAN + 2 * g
                    if g + 1 < SG:
                        decays(g + 1)
                    yield T_SCAN + 2 * g + 1
                    group_out(g)
                for c in range(4):
                    yield T_Z + 4 * c
                    w = next_chunk()
                    out = fill("act")
                    ins = yield from row_products(out, hnT, w, tick=T_Z + 4 * c)
                    ins.then_inc(sem("act_full"), 1)
                    chunk_used("act")
                yield T_YT
                lane.need("y_ready")
                for c in range(4):
                    transposes(y[:, c * CW:(c + 1) * CW], 4, "dve")
                yTk = yT.rearrange("p (half k) t -> p half k t", half=2)
                for n in range(2):
                    for half in range(2):
                        at = T_OUT1 + 4 * (2 * n + half)
                        yield at
                        if n == half == 0:
                            emptied("dve")
                        if half == 0:
                            out = fill("dve")
                        w = next_chunk()
                        ins = yield from row_products(out, yTk[:, half], w, half == 0, half == 1, tick=at)
                        if half:
                            ins.then_inc(sem("dve_full"), 1)
                            chunk_used("dve")
                        else:
                            lane(ins)
                            pe.sem_inc(sem("chunks_free"), 1)

            def queries(layer, b, base):
                yield base + 1
                norm_transposes(b)
                emptied("act")
                for c in range(4):
                    at = base + T_Q + 4 * c
                    yield at
                    w = next_chunk()
                    out = fill("act")
                    ins = yield from column_products(out, w, at)
                    ins.then_inc(sem("act_full"), 1)
                    chunk_used("act")
                yield base + T_KEYS
                pe.wait_ge(sem("keys_loaded"), 16)
                emptied("act")
                for c in range(4):
                    if c == 2:
                        yield base + T_KEYS + 1
                    out = fill("act")
                    for j in range(4):
                        m = c * 4 + j
                        ins = pe.matmul(out[:, j * NK:(j + 1) * NK], qT[:, m], keysT[:, layer, m % 2],
                                        start=True, stop=True)
                    ins.then_inc(sem("act_full"), 1)

            def side(layer, b):
                yield from (mixer1 if layer else mixer0)(b)
                yield from queries(layer, b, T_END1 if layer else T_END0)

            def sum_slot(g, n):
                if n % GROUP == 0:
                    pe.wait_ge(sem("diag_ready"), g * 4 + (n // GROUP + 1))
                slot = n % RING
                for half in range(2):
                    ins = pe.matmul(acc[half], diag[:, slot], ring[:, slot, D + half * CW:D + (half + 1) * CW],
                                    start=False, stop=False, skip_group_check=True)
                ins.then_inc(sem("slots_free"), 1)

            def experts(phase, beside=None):
                if phase:
                    pe.wait_ge(sem("acc_read"), phase)
                b = phase % NBLK
                for n in range(2):
                    pe.matmul(acc[n], zrow[0:1, :], hn[0:1, b, n * CW:(n + 1) * CW], start=True, stop=False,
                              skip_group_check=True)
                first = phase * STEPS
                looped = first + UNROLLED[phase]
                if beside:
                    total = UNROLLED[phase] * BODY
                    for n in range(total + GROUP):
                        if n >= GROUP:
                            sum_slot(first + (n - GROUP) // BODY, (n - GROUP) % BODY)
                        if n < total:
                            beside.upto(pace(phase, n))
                if looped < first + STEPS:
                    with pe.Fori(looped, first + STEPS) as g:
                        for n in range(BODY):
                            sum_slot(g, n)
                for n in range(2):
                    ins = pe.matmul(acc[n], zrow[0:1, :], hn[0:1, b, n * CW:(n + 1) * CW], start=False, stop=True,
                                    skip_group_check=True)
                ins.then_inc(sem("acc_full"), 1)
                if beside:
                    beside.finish()

            pe.sem_inc(sem("chunks_free"), NWB)
            pe.sem_inc(sem("slots_free"), RING)
            pe.wait_ge(sem("consts_loaded"), 16)
            pe.wait_ge(sem("zero_row"), 1)
            Side(side(0, 0)).finish()
            experts(0, Side(side(0, 1)))
            experts(1, Side(side(1, 0)))
            experts(2, Side(side(1, 1)))
            experts(3)

        @block.scalar
        def _(act):
            lane = Lane(act, "act_own")
            banks_in = Emptier(act, "act", act_banks)

            def f(out, in_, func, name=None, **more):
                lane(act.activation(out, in_, func, **more), name)

            def empty(out, func=ACT.Copy, pattern=None, cols=CW, **dims):
                src = banks_in.take()[:, 0:cols]
                f(out, src.rearrange(pattern, **dims) if pattern else src, func, "act_emptied")

            def inverse_root(n):
                lane.need("root_asked")
                f(stat[:, 16:16 + n], stat[:, 0:n], ACT.Ln)
                f(stat[:, 32:32 + n], stat[:, 16:16 + n], ACT.Exp, scale=-0.5)
                lane.tell("root_given")

            def norm(base):
                inverse_root(1)
                yield base + 2
                for n in range(2):
                    empty(hnT[:, 4 * n:4 * n + 4], pattern="p (k t) -> p k t", k=4)

            def mixer0(b):
                yield from norm(0)
                yield T_IN0 + 4
                empty(pool_in[:, b])
                yield T_IN0 + 13
                inverse_root(2 * HEADS)
                yield T_IN0 + 16
                empty(v_rows[:, b])
                empty(qT_att, pattern="p (n t) -> p n t", n=4)
                empty(kT[:, :, b * P:(b + 1) * P], pattern="p (n t) -> p n t", n=4)
                yield T_IN0 + 17
                empty(mixedT, pattern="p (n c) -> p n c", n=NWIN)
                yield T_ATT - 1

                def exp_scores(hd):
                    lane.need("scores_biased")
                    part = probs[:, hd % 3, 0:(b + 1) * P]
                    f(part, part, ACT.Exp, bias=stat[:, 64 + hd % 3:65 + hd % 3],
                      accum_out=stat[:, 68 + hd % 3:69 + hd % 3])
                    lane.tell("scores_exp")

                exp_scores(0)
                for hd in range(HEADS):
                    yield T_ATT + 2 * hd
                    if hd + 1 < HEADS:
                        exp_scores(hd + 1)
                    yield T_ATT + 2 * hd + 1
                    empty(probsT[:, hd % 2, 0:b + 1], pattern="p (j q) -> p j q", cols=(b + 1) * P, j=b + 1)
                    lane.tell("probs_taken")
                    if hd % 2:
                        empty(mixT[:, NWIN + hd // 2], cols=P)

            def mixer1(b):
                yield from norm(0)
                yield T_NORM + 1
                lane.need("dt_abs")
                f(dtv[:, 6], dtv[:, 2], ACT.Exp, scale=-1.0)
                f(dtv[:, 6], dtv[:, 6], ACT.Ln, bias=1.0)
                lane.tell("dt_log")

                def silu(d):
                    act.wait_ge(sem("conv_done"), 8 * b + d + 1)
                    if d < 4:
                        f(xT[:, d % 2], xT[:, d % 2], ACT.Silu)
                    else:
                        f(bcT[:, (d - 4) * 4:(d - 3) * 4].rearrange("p g t -> p (g t)"), xT[:, d % 2], ACT.Silu)
                    lane.tell("conv_ready" if d < 6 else "c_ready")

                for c in range(8):
                    yield T_IN1 + 4 * c + 4
                    empty(conv_in[:, c % 2, :, TAPS - 1:], pattern="p (j t) -> p j t", j=4)
                    lane.tell("conv_loaded")
                    if c == 1:
                        lane.need("sums_ready")
                        f(dtv[:, 5:7].rearrange("p n c -> p (n c)"), dtv[:, 3:5].rearrange("p n c -> p (n c)"), ACT.Exp)
                        lane.tell("decay_factors")
                    if 1 <= c < 7:
                        d = c - 1
                        empty(x_rows[:, d * CW:(d + 1) * CW] if d < 4 else b_rows[:, (d - 4) * CW:(d - 3) * CW])
                        lane.tell("conv_rows")
                    yield T_IN1 + 4 * c + 6
                    silu(c)
                lane.tell("bc_ready")
                if b + 1 < NBLK:
                    for half in range(4):
                        yield T_CB + 2 + half
                        empty(state[:, 2 * half:2 * half + 2], pattern="p (g c) -> p g c", g=2)
                for g in range(SG):
                    yield T_SCAN + 2 * g
                    lane.need("decay_args")
                    f(decay[:, g % 2], decay[:, g % 2], ACT.Exp)
                    lane.tell("decay_exp")
                for c in range(4):
                    yield T_Z + 4 * c + 4
                    if c >= 2:
                        act.wait_ge(sem("z_used"), 4 * b + c - 1)
                    empty(xT[:, c % 2], ACT.Silu)
                    lane.tell("z_ready")
                yield T_Z + 17
                inverse_root(SG)

            def queries(layer, b, base):
                yield base
                yield from norm(base)
                if layer == 0 and b == NBLK - 1:
                    act.dma_start(gains, gain_rows(1)).then_inc(sem("gains_loaded"), 16)
                for c in range(4):
                    yield base + T_Q + 4 * c + 4
                    empty(qT[:, 4 * c:4 * c + 4], pattern="p (m t) -> p m t", m=4)
                for c in range(4):
                    yield base + T_KEYS + c // 2
                    empty(scores[:, 4 * c:4 * c + 4], pattern="p (m k) -> p m k", m=4)
                    lane.tell("scores_ready")
                yield base + T_TOP + 20
                lane.need("best_ready")
                f(expd, expd, ACT.Exp)
                lane.tell("best_exp")

            def side(layer, b):
                yield from (mixer1 if layer else mixer0)(b)
                yield from queries(layer, b, T_END1 if layer else T_END0)

            def take_gelu(g, q):
                cols = slice(q * GROUP, (q + 1) * GROUP)
                act.wait_ge(sem("dot_done"), g * BODY + (q + 1) * GROUP)
                act.activation(acts[:, cols], dots[:, cols], ACT.Gelu).then_inc(sem("gelu_done"), 1)

            def make_diagonals(g, q):
                act.wait_ge(sem("coef_done"), g * 4 + (q + 1))
                act.wait_ge(sem("slots_free"), g * BODY + (q + 1) * GROUP)
                for s in range(GROUP):
                    ins = act.activation(diag[:, (q % 2) * GROUP + s], ident, ACT.Copy,
                                         scale=coefs[:, q * GROUP + s:q * GROUP + s + 1])
                ins.then_inc(sem("diag_ready"), 1)

            def experts(phase, beside=None):
                first = phase * STEPS
                looped = first + UNROLLED[phase]
                if beside:
                    for n in range(UNROLLED[phase] * BODY):
                        g, q = first + n // BODY, n % BODY // GROUP
                        if n % GROUP == GROUP - 1:
                            take_gelu(g, q)
                        beside.upto(pace(phase, n))
                        if n % GROUP == GROUP - 1:
                            make_diagonals(g, q)
                if looped < first + STEPS:
                    with act.Fori(looped, first + STEPS) as g:
                        for q in range(BODY // GROUP):
                            take_gelu(g, q)
                            make_diagonals(g, q)
                if beside:
                    beside.finish()

            act.wait_ge(sem("consts_loaded"), 16)
            act.wait_ge(sem("rows_loaded"), 16)
            f(eA, a_log, ACT.Exp)
            Side(side(0, 0)).finish()
            experts(0, Side(side(0, 1)))
            experts(1, Side(side(1, 0)))
            experts(2, Side(side(1, 1)))
            experts(3)

        @block.vector
        def _(dve):
            lane = Lane(dve, "dve_own")
            banks_in = Emptier(dve, "dve", dve_banks)

            def tt(out, in0, in1, op=ALU.mult, name=None):
                lane(dve.tensor_tensor(out, in0, in1, op), name)

            def ts(out, in0, s1, s2, op0, op1=None, name=None):
                more = () if op1 is None else (op1,)
                lane(dve.tensor_scalar(out, in0, s1, s2, op0, *more), name)

            def stt(out, in0, scalar, in1, op0, op1, name=None):
                lane(dve.scalar_tensor_tensor(out, in0, scalar, in1, op0, op1), name)

            def add_to_stream(b, n, src, name):
                part = h[:, b, n * CW:(n + 1) * CW]
                tt(part, part, src, ALU.add, name)

            def inverse_root(n):
                v, r, t = stat[:, 0:n], stat[:, 32:32 + n], stat[:, 48:48 + n]
                lane.tell("root_asked")
                lane.need("root_given")
                tt(t, r, r)
                tt(t, t, v)
                ts(t, t, -0.5, 1.5, ALU.mult, ALU.add)
                tt(r, r, t)

            def norm(layer, which, b):
                dve.wait_ge(sem("gains_loaded"), 16 * (layer + 1))
                lane(dve.tensor_tensor_reduce(out=hn[:, b], in0=h[:, b], in1=h[:, b], scale=1.0, scalar=0.0,
                                              op0=ALU.mult, op1=ALU.add, accum_out=stat[:, 0:1]))
                ts(stat[:, 0:1], stat[:, 0:1], 1.0 / D, EPS, ALU.mult, ALU.add)
                inverse_root(1)
                stt(hn[:, b], h[:, b], stat[:, 32:33], gains[:, which], ALU.mult, ALU.mult)
                lane.tell("hn_ready")

            def mixer0(b):
                norm(0, 0, b)
                for i in range(2):
                    yield T_IN0 + 8 + 4 * i
                    lane(dve.tensor_copy(qk[:, i], banks_in.take()), "dve_emptied")
                dve.wait_ge(sem("rows_loaded"), 16)
                flat = qk.rearrange("p i c -> p (i c)")
                heads = flat.rearrange("p (m e) -> p m e", e=HD)
                tt(qk_sq, flat, flat)
                yield T_IN0 + 13
                lane(dve.reduce_sum(stat[:, 0:16], qk_sq.rearrange("p (m e) -> p m e", e=HD), AX))
                ts(stat[:, 0:16], stat[:, 0:16], 1.0 / HD, EPS, ALU.mult, ALU.add)
                inverse_root(2 * HEADS)
                yield T_IN0 + 14
                tt(heads, heads, stat[:, 32:48].unsqueeze(2).to_broadcast([P, 2 * HEADS, HD]))
                yield T_IN0 + 15
                for i in range(2):
                    part = qk[:, i].rearrange("p (m e) -> p m e", e=HD)
                    tt(part, part, qk_gain[:, i:i + 1].to_broadcast([P, HEADS, HD]))
                lane.tell("qk_ready")
                yield T_IN0 + 18
                dve.wait_ge(sem("cols_loaded"), 16)
                tt(mixT[:, 0:NWIN], banks_in.take().rearrange("p (n t) -> p n t", n=NWIN),
                   pool_scale.unsqueeze(2).to_broadcast([P, NWIN, P]), name="dve_emptied")
                yield T_ATT - 1
                dve.wait_ge(sem("bias_loaded"), 16)

                def bias_scores(hd):
                    if hd >= 3:
                        lane.need("probs_taken")
                    keys = (b + 1) * P
                    part = probs[:, hd % 3, 0:keys]
                    stt(part, banks_in.take()[:, 0:keys], HD ** -0.5, bias_t[:, hd, 2 * P - keys:],
                        ALU.mult, ALU.add, "dve_emptied")
                    top = stat[:, 64 + hd % 3:65 + hd % 3]
                    lane(dve.reduce_max(top, part, AX))
                    ts(top, top, -1.0, None, ALU.mult)
                    lane.tell("scores_biased")

                bias_scores(0)
                for hd in range(HEADS):
                    yield T_ATT + 2 * hd
                    if hd + 1 < HEADS:
                        bias_scores(hd + 1)
                    lane.need("scores_exp")
                    total = stat[:, 68 + hd % 3:69 + hd % 3]
                    part = probs[:, hd % 3, 0:(b + 1) * P]
                    lane(dve.reciprocal(total, total))
                    ts(part, part, total, None, ALU.mult)
                    lane.tell("probs_ready")
                for n in range(3):
                    lane.need("probs_taken")
                for n in range(2):
                    yield T_OUT0 + 4 * n + 4
                    add_to_stream(b, n, banks_in.take(), "dve_emptied")

            def mixer1(b):
                norm(1, 0, b)
                yield T_NORM + 1
                tt(dtv[:, 0], banks_in.take()[:, 0:SH], dt_bias, ALU.add, "dve_emptied")
                stt(dtv[:, 2], dtv[:, 0], -1.0, dtv[:, 0], ALU.mult, ALU.max)
                lane.tell("dt_abs")
                yield T_NORM + 2
                lane.need("dt_log")
                stt(dtv[:, 0], dtv[:, 0], 0.0, dtv[:, 6], ALU.max, ALU.add)
                stt(dtv[:, 1], dtv[:, 0], -1.0, eA, ALU.mult, ALU.mult)
                lane.tell("da_ready")
                for c in range(8):
                    yield T_IN1 + 4 * c + 4
                    if c >= 2:
                        lane.need("conv_rows")
                    lane.need("conv_loaded")
                    tiles = conv_in[:, c % 2]
                    tails = carry[:, 4 * c:4 * c + 4]
                    if b:
                        lane(dve.tensor_copy(tiles[:, :, 0:TAPS - 1], tails))
                    else:
                        lane(dve.memset(tiles[:, :, 0:TAPS - 1], 0.0))
                        lane(dve.tensor_copy(tails, tiles[:, :, P:]))
                    if c == 1:
                        lane(dve.tensor_copy(dtv[:, 3:5].rearrange("p n c -> p (n c)"), banks_in.take()[:, 0:2 * SH]),
                             "dve_emptied")
                        lane.tell("sums_ready")
                    for j in range(4):
                        t = 4 * c + j
                        out = xT[:, c % 2, j * P:(j + 1) * P]
                        ts(out, tiles[:, j, 0:P], taps[:, t, 0:1], conv_b[:, t:t + 1], ALU.mult, ALU.add)
                        for tap in range(1, TAPS):
                            stt(out, tiles[:, j, tap:tap + P], taps[:, t, tap:tap + 1], out, ALU.mult, ALU.add)
                        if j == 1:
                            yield T_IN1 + 4 * c + 5
                    lane.tell("conv_done")
                by_head = "p (h e) -> p h e"
                step = dtv[:, 0].unsqueeze(2).to_broadcast([P, SH, SP_])
                yield T_CB - 2
                tt(xdt.rearrange(by_head, h=SH), x_rows.rearrange(by_head, h=SH), step)
                yield T_CB - 1
                lane.need("decay_factors")
                if b + 1 < NBLK:
                    tt(y.rearrange(by_head, h=SH), xdt.rearrange(by_head, h=SH),
                       dtv[:, 6].unsqueeze(2).to_broadcast([P, SH, SP_]))
                    lane.tell("xdtw_ready")
                for half in range(2):
                    yield T_CB + 1 + half
                    tt(cb[:, 4 * half:4 * half + 4], banks_in.take().rearrange("p (g l) -> p g l", g=4),
                       tri.unsqueeze(1).to_broadcast([P, 4, P]), name="dve_emptied")
                yield T_CB + 6
                if b + 1 < NBLK:
                    lane.need("xdtw_taken")
                tt(y.rearrange(by_head, h=SH), x_rows.rearrange(by_head, h=SH),
                   d_skip.unsqueeze(2).to_broadcast([P, SH, SP_]))

                def decay_args(g):
                    out = banks_in.take()
                    for r in range(HPG):
                        head = g * HPG + r
                        ts(decay[:, g % 2, r], out[:, r * P:(r + 1) * P], dtv[:, 3, head:head + 1], 0.0,
                           ALU.subtract, ALU.min, "dve_emptied" if r == HPG - 1 else None)
                    lane.tell("decay_args")

                def group_out(g):
                    out = banks_in.take()
                    part = y[:, g * GW:(g + 1) * GW]
                    if b:
                        tt(y_tmp.rearrange(by_head, h=HPG), out[:, GW:2 * GW].rearrange(by_head, h=HPG),
                           dtv[:, 5, g * HPG:(g + 1) * HPG].unsqueeze(2).to_broadcast([P, HPG, SP_]))
                        tt(part, part, y_tmp, ALU.add)
                    tt(part, part, out[:, 0:GW], ALU.add, "dve_emptied")

                decay_args(0)
                for g in range(SG):
                    yield T_SCAN + 2 * g
                    if g:
                        group_out(g - 1)
                    if g + 1 < SG:
                        decay_args(g + 1)
                    lane.need("decay_exp")
                    tt(decay[:, g % 2], decay[:, g % 2], cb[:, g:g + 1].to_broadcast([P, HPG, P]))
                    lane.tell("weights_ready")
                yield T_SCAN + 2 * SG
                group_out(SG - 1)
                for c in range(4):
                    yield T_Z + 4 * c + 4
                    lane.need("z_ready")
                    part = y[:, c * CW:(c + 1) * CW]
                    tt(part, part, xT[:, c % 2])
                    lane.tell("z_used")
                yield T_Z + 17
                grouped = y.rearrange("p (g c) -> p g c", g=SG)
                tt(x_rows, y, y)
                lane(dve.reduce_sum(stat[:, 0:SG], x_rows.rearrange("p (g c) -> p g c", g=SG), AX))
                ts(stat[:, 0:SG], stat[:, 0:SG], 1.0 / GW, EPS, ALU.mult, ALU.add)
                inverse_root(SG)
                yield T_Z + 18
                tt(grouped, grouped, stat[:, 32:32 + SG].unsqueeze(2).to_broadcast([P, SG, GW]))
                lane.tell("y_ready")
                yield T_YT
                for c in range(4):
                    tt(yT[:, 4 * c:4 * c + 4], banks_in.take().rearrange("p (k t) -> p k t", k=4),
                       gate_gain[:, 4 * c:4 * c + 4].unsqueeze(2).to_broadcast([P, 4, P]), name="dve_emptied")
                for n in range(2):
                    yield T_OUT1 + 8 * n + 8
                    add_to_stream(b, n, banks_in.take(), "dve_emptied")

            def top16(src, values, places):
                lane(dve.max(values[:, 0:8], src))
                lane(dve.max_index(places[:, 0:8], values[:, 0:8], src))
                lane(dve.match_replace(src, values[:, 0:8], src, NEG))
                lane(dve.max(values[:, 8:16], src))
                lane(dve.max_index(places[:, 8:16], values[:, 8:16], src))

            def routing(layer, b, base):
                yield base
                norm(layer, 1, b)
                for m in range(M16):
                    yield base + T_KEYS + 1 + m * 8 // M16
                    if m % 4 == 0:
                        lane.need("scores_ready")
                    cols = slice(m * TOPK, (m + 1) * TOPK)
                    top16(scores[:, m], top_s[:, cols], top_i[:, cols])
                halves = top_s.rearrange("p (h i a) -> p i h a", i=2, a=TOPK)
                grid = cand.rearrange("p h (a b) -> p h a b", a=TOPK)
                for hd in range(PH):
                    yield base + T_TOP + 8 + hd * 3 // 4
                    a = halves[:, 0, hd].unsqueeze(2).to_broadcast([P, TOPK, TOPK])
                    c = halves[:, 1, hd].unsqueeze(1).to_broadcast([P, TOPK, TOPK])
                    tt(grid[:, hd], a, c, ALU.add)
                    cols = slice(hd * TOPK, (hd + 1) * TOPK)
                    top16(cand[:, hd], best[:, cols], best_pos[:, cols])
                yield base + T_TOP + 14
                ts(pos_hi, best_pos, 4, None, ALU.logical_shift_right)
                ts(pos_lo, best_pos, 15, None, ALU.bitwise_and)
                lane(dve.tensor_copy(pos_f[:, 0], pos_hi))
                lane(dve.tensor_copy(pos_f[:, 1], pos_lo))
                lane(dve.tensor_copy(top_if, top_i))
                keys = top_if.rearrange("p (h i a) -> p i h a", i=2, a=TOPK)
                hot = onehot.rearrange("p (h s a) -> p h s a", h=PH, s=TOPK)
                hot_flat = onehot.rearrange("p (n a) -> p n a", a=TOPK)
                for i in range(2):
                    yield base + T_TOP + 15 + 2 * i
                    tt(hot_flat, pos_f[:, i].unsqueeze(2).to_broadcast([P, SLOTS, TOPK]),
                       iota16.unsqueeze(1).to_broadcast([P, SLOTS, TOPK]), ALU.is_equal)
                    yield base + T_TOP + 16 + 2 * i
                    tt(hot, hot, keys[:, i].unsqueeze(2).to_broadcast([P, PH, TOPK, TOPK]))
                    lane(dve.reduce_sum(picked[:, i], hot_flat, AX))
                yield base + T_TOP + 20
                stt(pos_f[:, 0], picked[:, 0], float(NK), picked[:, 1], ALU.mult, ALU.add)
                lane(dve.tensor_copy(idx[:, b * SLOTS:(b + 1) * SLOTS], pos_f[:, 0]))
                lane.tell("idx_ready")
                by_head = best.rearrange("p (h s) -> p h s", h=PH)
                exps = expd.rearrange("p (h s) -> p h s", h=PH)
                tt(exps, by_head, by_head[:, :, 0:1].to_broadcast([P, PH, TOPK]), ALU.subtract)
                lane.tell("best_ready")
                lane.need("best_exp")
                lane(dve.reduce_sum(stat[:, 72:72 + PH], exps, AX))
                lane(dve.reciprocal(stat[:, 72:72 + PH], stat[:, 72:72 + PH]))
                tt(gate[:, b * SLOTS:(b + 1) * SLOTS].rearrange("p (h s) -> p h s", h=PH), exps,
                   stat[:, 72:72 + PH].unsqueeze(2).to_broadcast([P, PH, TOPK]))

            def side(layer, b):
                yield from (mixer1 if layer else mixer0)(b)
                yield from routing(layer, b, T_END1 if layer else T_END0)

            def dot(phase, g, n):
                slot = n % RING
                dve.wait_ge(sem(f"rows_in{slot}"), g * 32 + 16 * (n // RING + 1))
                dve.tensor_tensor_reduce(out=ring[:, slot, 0:D], in0=ring[:, slot, 0:D], in1=hn[:, phase % NBLK],
                                         scale=1.0, scalar=0.0, op0=ALU.mult, op1=ALU.add,
                                         accum_out=dots[:, n:n + 1]).then_inc(sem("dot_done"), 1)
                dve.wait_ge(sem("dot_done"), g * BODY + (n + 1))

            def coefficients(phase, g, q):
                dve.wait_ge(sem("gelu_done"), g * 4 + (q + 1))
                cols = slice(q * GROUP, (q + 1) * GROUP)
                at = g * BODY + (q * GROUP - phase // NBLK * NBLK * SLOTS)
                dve.tensor_tensor(coefs[:, cols], acts[:, cols], gate[:, bass.ds(at, GROUP)],
                                  ALU.mult).then_inc(sem("coef_done"), 1)

            def experts(phase, beside=None):
                first = phase * STEPS
                looped = first + UNROLLED[phase]
                if beside:
                    for n in range(UNROLLED[phase] * BODY):
                        g = first + n // BODY
                        dot(phase, g, n % BODY)
                        beside.upto(pace(phase, n))
                        if n % GROUP == GROUP - 1:
                            coefficients(phase, g, n % BODY // GROUP)
                if looped < first + STEPS:
                    with dve.Fori(looped, first + STEPS) as g:
                        for n in range(BODY):
                            dot(phase, g, n)
                            if n % GROUP == GROUP - 1:
                                coefficients(phase, g, n // GROUP)
                if beside:
                    beside.finish()
                dve.wait_ge(sem("acc_full"), phase + 1)
                for n in range(2):
                    add_to_stream(phase % NBLK, n, acc[n], None)
                lane.tell("acc_read")
                if phase // NBLK == DEPTH - 1:
                    lane.tell("out_ready")

            dve.wait_ge(sem("consts_loaded"), 16)
            dve.wait_ge(sem("x_loaded"), 16)
            Side(side(0, 0)).finish()
            experts(0, Side(side(0, 1)))
            experts(1, Side(side(1, 0)))
            experts(2, Side(side(1, 1)))
            experts(3)


def chunked(w):
    k, n = w.shape
    w = w.reshape(k // D, KD, P, n // CW, CW)
    return w.transpose(3, 0, 2, 1, 4).reshape(-1, P, CH)


def tiles_last(v):
    return v.reshape(-1, P).T


def kernel(**inputs):
    import concourse.bacc as bacc
    from concourse.bass_utils import run_bass_kernel_spmd

    a = {k: np.asarray(v) for k, v in inputs.items()}
    w_in = a["ssm_w_in"][0]
    pool_first = a["even_w_in"][0]
    consts, bands = shape_constants()
    weights = [chunked(pool_first), chunked(a["even_w_out"][0]), chunked(a["peer_w_q"][0]),
               chunked(w_in[:, SI:SI + XBC]), chunked(w_in[:, 0:SI]), chunked(a["ssm_w_out"][0]),
               chunked(a["peer_w_q"][1])]
    conv_w = a["conv_w"][0].reshape(TAPS, XT, P).transpose(2, 1, 0).reshape(P, XT * TAPS)
    arrays = {
        "x": a["x"].reshape(SEQ, D),
        "gains": np.stack([a["attn_norm"], a["ffn_norm"]], axis=1),
        "weights": np.concatenate(weights, axis=0),
        "dt_w": w_in[:, SI + XBC:],
        "rows": np.concatenate([a["q_gain"][0], a["k_gain"][0], a["dt_bias"][0], a["a_log"][0],
                                a["d_skip"][0]])[None, :],
        "cols": np.concatenate([tiles_last(a["pool_scale"][0]), conv_w, tiles_last(a["conv_b"][0]),
                                tiles_last(a["gate_gain"][0])], axis=1),
        "pool_w": a["pool_w"][0],
        "keysT": a["peer_sub_keys"].transpose(0, 1, 3, 2),
        "experts0": np.concatenate([a["peer_u"][0], a["peer_v"][0]], axis=1),
        "experts1": np.concatenate([a["peer_u"][1], a["peer_v"][1]], axis=1),
        "consts": consts, "bands": bands, "bias": attention_bias(),
    }
    arrays = {"in_" + k: np.ascontiguousarray(v) for k, v in arrays.items()}
    nc = bacc.Bacc("TRN2", target_bir_lowering=False, num_devices=1)
    io = {k[3:]: nc.dram_tensor(k, v.shape, mybir.dt.from_np(v.dtype), kind="ExternalInput").ap()
          for k, v in arrays.items()}
    io["out"] = nc.dram_tensor("out", (SEQ, D), mybir.dt.float32, kind="ExternalOutput").ap()
    build_trunk(nc, io)
    r = run_bass_kernel_spmd(nc, [arrays], core_ids=[0])
    return r.results[0]["out"].reshape(1, SEQ, D)
```

```python
import math
from contextlib import ExitStack

import numpy as np

import concourse.bass as bass
from concourse import mybir

P = 128
D = 1024
KD = D // P
SEQ = 256
NBLK = SEQ // P
DEPTH = 2
POOL_WINDOWS = (2, 4, 8, 16)
NWIN = len(POOL_WINDOWS)
POOL_W = D // 8 * NWIN
HEADS, HD = 8, 64
AW = HEADS * HD
BRANCHES = ((128, 1), (512, 4), (2048, 16))
EPS = 1e-6
SH, SP_, SG, SN, TAPS = 32, 64, 8, 128, 4
SI = SH * SP_
DBUF = 3
HPG = SH // SG
GW = HPG * SP_
XBC = SI + 2 * SG * SN
XT = XBC // P
PH, NK, HALF, TOPK = 8, 128, 128, 16
M16 = 2 * PH
WHOLE = TOPK // 2
CAND = WHOLE * TOPK + TOPK - WHOLE
SLOTS = PH * TOPK
CW = 512
CH = KD * CW
NEG = -1.0e30

RING = 8
GROUP = 2
DIAGS = 2 * GROUP
BODY = 2 * RING
GROUPS = BODY // GROUP
STEPS = SLOTS // BODY
assert BODY == TOPK

NWB = 2
L0_CHUNKS = 4 + 2 + 4
L1_CHUNKS = 8 + 4 + 4 + 4
CHUNKS = (L0_CHUNKS, L1_CHUNKS)
KEEP = 1

T_IN0 = 3
T_ATT = T_IN0 + 14
T_OUT0 = T_ATT + 16
T_END0 = T_OUT0 + 8 + 1
T_IN1 = 5
T_CB = T_IN1 + 32 + 4
T_SCAN = T_CB + 6
T_YT = T_SCAN + 30
T_OUT1 = T_YT + 3
T_END1 = T_OUT1 + 16 + 1
T_END = (T_END0, T_END1)
T_Q = 3
T_TOP = T_Q + 3
T_PART = 4
T_FIRST = T_TOP + T_PART
T_ROUTED = T_TOP + PH * T_PART

PHASES = DEPTH * NBLK
START = [0]
for _phase in range(PHASES):
    START.append(START[-1] + T_END[_phase // NBLK] + T_ROUTED)
UNROLLED = {0: STEPS, 1: STEPS, 2: STEPS, 3: 4}
ROUTED_BY = (28, 20, 20, 44)
KNOWN_BY = 120
ON_THE_WAY = (((T_OUT0, 0.65),), ((T_CB, 0.38), (T_YT, 0.68)))
KNOTS = [(0, T_END0 + T_FIRST)]
for _phase in range(1, PHASES):
    _layer, _slot, _from = _phase // NBLK, (_phase - 1) * SLOTS, ROUTED_BY[_phase - 1]
    KNOTS.append((_slot + _from, START[_phase]))
    for _tick, _share in ON_THE_WAY[_layer]:
        KNOTS.append((_slot + _from + _share * (KNOWN_BY - _from), START[_phase] + _tick))
    KNOTS.append((_slot + KNOWN_BY, START[_phase] + T_END[_layer] + T_FIRST))
KNOTS.append(((PHASES - 1) * SLOTS + ROUTED_BY[PHASES - 1], START[PHASES]))

C_ID, C_TRI, C_STRI, C_IOTA = 0, P, 2 * P, 3 * P
C_END = C_IOTA + TOPK


def shape_constants():
    c = np.zeros((P, C_END), np.float32)
    row, col = np.arange(P)[:, None], np.arange(P)[None, :]
    c[:, C_ID:C_ID + P] = row == col
    c[:, C_TRI:C_TRI + P] = row <= col
    c[:, C_STRI:C_STRI + P] = row > col
    c[:, C_IOTA:] = np.arange(TOPK)
    bands = np.zeros((P, 3, NWIN, P), np.float32)
    for n, w in enumerate(POOL_WINDOWS):
        lag = col - row
        first = ((lag >= 0) & (lag < w)) / np.minimum(col + 1, w) - (lag == 0)
        later = ((lag >= 0) & (lag < w)) / w - (lag == 0)
        before = ((lag + P >= 0) & (lag + P < w)) / w
        for k, band in enumerate((first, later, before)):
            bands[:, k, n] = band
    return c, bands.reshape(P, -1)


def attention_bias():
    dist = np.arange(P)[:, None] + P - np.arange(2 * P)[None, :]
    count = np.zeros((P, 2 * P))
    for window, dilation in BRANCHES:
        count += (dist >= 0) & (dist <= window) & (dist % dilation == 0)
    logs = np.where(count > 0, np.log(np.maximum(count, 1)), NEG)
    slopes = 2.0 ** (-8.0 * np.arange(1, HEADS + 1) / HEADS)
    bias = -slopes[None, :, None] * dist[:, None, :] + logs[:, None, :]
    return np.ascontiguousarray(bias.reshape(P, HEADS * 2 * P).astype(np.float32))


def build_trunk(nc, io):
    f32, u32 = mybir.dt.float32, mybir.dt.uint32
    ALU = mybir.AluOpType
    ACT = mybir.ActivationFunctionType
    AX = mybir.AxisListType.X

    ctx = ExitStack()
    with ctx:
        def sb(name, cols, dt=f32):
            return ctx.enter_context(nc.sbuf_tensor(name, [P, cols], dt))[:, :]

        def bank(name):
            return ctx.enter_context(nc.psum_tensor(name, [P, CW], f32))[:, :]

        sems = {}

        def sem(name):
            if name not in sems:
                sems[name] = ctx.enter_context(nc.semaphore(name))
            return sems[name]

        h = sb("h", NBLK * D).rearrange("p (b d) -> p b d", b=NBLK)
        hn = sb("hn", NBLK * D).rearrange("p (b d) -> p b d", b=NBLK)
        hnT = sb("hnT", KD * P).rearrange("p (k t) -> p k t", k=KD)
        gains = sb("gains", 2 * D).rearrange("p (n d) -> p n d", d=D)
        wbuf = sb("wbuf", NWB * CH).rearrange("p (n k c) -> p n k c", n=NWB, k=KD)
        kept = sb("kept", KEEP * CH).rearrange("p (n k c) -> p n k c", n=KEEP, k=KD)
        ring = sb("ring", RING * 2 * D).rearrange("p (r d) -> p r d", r=RING)
        cst = sb("cst", C_END)
        keysT = sb("keysT", DEPTH * 2 * NK).rearrange("p (l i k) -> p l i k", l=DEPTH, i=2)
        rowc = sb("rowc", 2 * HD + 3 * SH)
        colc = sb("colc", NWIN + XT * TAPS + XT + 16)
        dtw = sb("dtw", KD * SH).rearrange("p (k c) -> p k c", k=KD)
        diag = sb("diag", DIAGS * P).rearrange("p (n c) -> p n c", c=P)
        dots = sb("dots", BODY)
        acts = sb("acts", BODY)
        coefs = sb("coefs", BODY)
        idx_now = sb("idx_now", BODY, u32)
        idx = sb("idx", NBLK * SLOTS, u32)
        gate = sb("gate", NBLK * SLOTS)
        stat = sb("stat", 128)
        norm_root = stat[:, 127:128]
        eA = sb("eA", SH)

        ident = cst[:, C_ID:C_ID + P]
        tri = cst[:, C_TRI:C_TRI + P]
        stri = cst[:, C_STRI:C_STRI + P]
        iota16 = cst[:, C_IOTA:C_IOTA + 16]

        qk_gain = rowc[:, 0:2 * HD].rearrange("p (i e) -> p i e", i=2)
        dt_bias, a_log, d_skip = (rowc[:, 2 * HD + n * SH:2 * HD + (n + 1) * SH] for n in range(3))
        pool_scale = colc[:, 0:NWIN]
        taps = colc[:, NWIN:NWIN + XT * TAPS].rearrange("p (t j) -> p t j", j=TAPS)
        conv_b = colc[:, NWIN + XT * TAPS:NWIN + XT * TAPS + XT]
        gate_gain = colc[:, NWIN + XT * TAPS + XT:]

        SCRATCH = 14176
        ROUTING = 7008
        scratch = sb("scratch", SCRATCH)

        class Carve:
            def __init__(self, start=0, end=SCRATCH):
                self.at, self.end = start, end

            def __call__(self, size, pattern=None, **dims):
                part = scratch[:, self.at:self.at + size]
                self.at += size
                assert self.at <= self.end, self.at
                return part.rearrange(pattern, **dims) if pattern else part

        cut = Carve(end=ROUTING)
        qk = cut(2 * AW, "p (i c) -> p i c", i=2)
        qk_sq = cut(2 * AW)
        qT_att = cut(4 * P, "p (n t) -> p n t", n=4)
        probs = cut(2 * CW, "p (n c) -> p n c", n=2)
        probsT = cut(CW)
        mixedT = cut(NWIN * P, "p (n c) -> p n c", c=P)
        mixT = cut(8 * P, "p (k t) -> p k t", k=8)
        cut = Carve(ROUTING)
        bias_t = cut(HEADS * 2 * P, "p (h k) -> p h k", h=HEADS)
        bands = cut(3 * NWIN * P, "p (k n c) -> p k n c", k=3, n=NWIN)
        pool_w = cut(NWIN * P, "p (n c) -> p n c", c=P)
        pool_in = cut(NBLK * AW, "p (b c) -> p b c", b=NBLK)
        v_rows = cut(NBLK * AW, "p (b c) -> p b c", b=NBLK)
        kT = cut(4 * SEQ, "p (n t) -> p n t", n=4)

        cut = Carve()
        conv_in = cut(2 * 4 * (P + TAPS - 1), "p (n j t) -> p n j t", n=2, j=4)
        cut.at = 0
        decay = cut(DBUF * CW, "p (n r l) -> p n r l", n=DBUF, r=HPG)
        xT = cut(2 * CW, "p (n c) -> p n c", n=2)
        bcT = cut(2 * SG * P, "p (g t) -> p g t", g=2 * SG)
        x_rows = cut(SI)
        b_rows = cut(SG * SN)
        xdt = cut(SI)
        dtv = cut(8 * SH, "p (n c) -> p n c", n=8)
        y_tmp = b_rows[:, 0:GW]
        yT = bcT
        cb = bcT[:, 0:SG]
        cut.at = max(cut.at, ROUTING)
        state = cut(SG * GW, "p (g c) -> p g c", g=SG)
        carry = cut(XT * (TAPS - 1), "p (t c) -> p t c", t=XT)
        y = cut(SI)

        cut = Carve(end=ROUTING)
        qT = cut(M16 * P, "p (m t) -> p m t", m=M16)
        scores = cut(M16 * NK, "p (m k) -> p m k", m=M16)
        squares = cut(D)
        cand = cut(CAND)
        onehot = cut(2 * TOPK * TOPK)
        top_s = cut(2 * TOPK)
        top_i = cut(2 * TOPK).bitcast(u32)
        top_if = cut(2 * TOPK)
        best = cut(TOPK)
        best_pos = cut(TOPK).bitcast(u32)
        pos_hi = cut(TOPK).bitcast(u32)
        pos_lo = cut(TOPK).bitcast(u32)
        pos_f = cut(3 * TOPK)
        picked = cut(2 * TOPK)
        expd = cut(TOPK)

        acc = [bank("acc0"), bank("acc1")]
        act_banks = [bank(f"act_bank{n}") for n in range(3)]
        dve_banks = [bank(f"dve_bank{n}") for n in range(3)]

        def gain_rows(layer, which):
            return io["gains"][layer, which:which + 1].to_broadcast([P, D])

        block = ctx.enter_context(nc.Block())

        class Lane:

            def __init__(self, eng, own):
                self.eng, self.own, self.count, self.seen = eng, own, {}, {}

            def start(self, instruction, name=None):
                name = name or self.own
                self.count[name] = self.count.get(name, 0) + 1
                instruction.then_inc(sem(name), 1)
                return name, self.count[name]

            def after(self, started):
                self.eng.wait_ge(sem(started[0]), started[1])

            def __call__(self, instruction, name=None):
                self.after(self.start(instruction, name))

            def tell(self, name):
                self.eng.sem_inc(sem(name), 1)

            def need(self, name):
                self.seen[name] = self.seen.get(name, 0) + 1
                self.eng.wait_ge(sem(name), self.seen[name])

        class Emptier:

            def __init__(self, eng, kind, banks):
                self.eng, self.kind, self.banks, self.n = eng, kind, banks, 0

            def take(self):
                self.eng.wait_ge(sem(self.kind + "_full"), self.n + 1)
                self.n += 1
                return self.banks[(self.n - 1) % 3]

        class Side:

            def __init__(self, steps):
                self.steps, self.tick = steps, 0

            def upto(self, tick):
                while self.tick <= tick:
                    self.tick = next(self.steps, math.inf)
                return self

        def head_groups(b):
            per = 4 // (b + 1)
            return [list(range(odd + 2 * at, HEADS, 2))[:per] for at in range(0, HEADS // 2, per) for odd in (0, 1)]

        def pace(phase, n):
            return float(np.interp(phase * SLOTS + n, *zip(*KNOTS)))

        def one_after_another(side):
            for phase in range(PHASES):
                for tick in side(*divmod(phase, NBLK)):
                    yield START[phase] + tick

        @block.sync
        def _(sp):
            sp.dma_start(h[:, 0], io["x"][0:P]).then_inc(sem("x_loaded0"), 16)
            sp.dma_start(gains[:, 0], gain_rows(0, 0)).then_inc(sem("gain_loaded0"), 16)
            sp.dma_start(cst, io["consts"]).then_inc(sem("consts_loaded"), 16)

            def chunk(slot, t, at):
                sp.wait_ge(sem("chunks_free"), t + 1)
                sp.dma_start(wbuf[:, slot].rearrange("p k c -> p (k c)"),
                             io["weights"][at].rearrange("n p c -> p (n c)")).then_inc(sem(f"chunk_in{slot}"), 16)

            def streamed_chunks(t, at, count):
                for peeled in range(t % NWB):
                    chunk((t + peeled) % NWB, t + peeled, slice(at + peeled, at + peeled + 1))
                pairs = (t + t % NWB, t + count - (t + count) % NWB)
                with sp.Fori(pairs[0] // NWB, pairs[1] // NWB) as pair:
                    for slot in range(NWB):
                        chunk(slot, pair * NWB + slot, bass.ds(pair * NWB + (slot + at - t), 1))
                if pairs[1] < t + count:
                    chunk(0, pairs[1], slice(at + pairs[1] - t, at + pairs[1] - t + 1))

            t = at = 0
            for layer in range(DEPTH):
                if layer:
                    sp.wait_ge(sem("kept_free"), layer)
                for n in range(KEEP):
                    sp.dma_start(kept[:, n].rearrange("p k c -> p (k c)"), io["weights"][at + n]
                                 ).then_inc(sem("kept_in"), 16)
                if layer == 0:
                    sp.dma_start(gains[:, 1], gain_rows(0, 1)).then_inc(sem("gain_loaded1"), 16)
                for b in range(NBLK):
                    streamed_chunks(t, at + KEEP, CHUNKS[layer] - KEEP)
                    t += CHUNKS[layer] - KEEP
                at += CHUNKS[layer]
            for b in range(NBLK):
                sp.wait_ge(sem("out_ready"), b + 1)
                sp.dma_start(io["out"][b * P:(b + 1) * P, :], h[:, b]).then_inc(sem("stored"), 16)
            sp.wait_ge(sem("stored"), 16 * NBLK)

        @block.gpsimd
        def _(pool):
            pool.dma_start(rowc, io["rows"].to_broadcast([P, 2 * HD + 3 * SH])).then_inc(sem("rows_loaded"), 16)
            pool.wait_ge(sem("chunk_in1"), 16)
            pool.dma_start(bands, io["bands"].rearrange("p (k n c) -> p k n c", k=3, n=NWIN)).then_inc(sem("bands_loaded"), 16)
            pool.dma_start(pool_w, io["pool_w"].rearrange("n c d -> c n d")).then_inc(sem("pool_w_loaded"), 16)
            pool.dma_start(colc, io["cols"]).then_inc(sem("cols_loaded"), 16)
            pool.dma_start(bias_t, io["bias"].rearrange("p (h k) -> p h k", h=HEADS)).then_inc(sem("bias_loaded"), 16)
            pool.dma_start(keysT, io["keysT"].rearrange("l i e k -> e l i k")).then_inc(sem("keys_loaded"), 16)
            pool.dma_start(h[:, 1], io["x"][P:2 * P]).then_inc(sem("x_loaded1"), 16)
            pool.dma_start(dtw, io["dt_w"].rearrange("(k p) c -> p k c", p=P)).then_inc(sem("dtw_loaded"), 16)

            def gather_step(layer, g):
                pool.wait_ge(sem("idx_ready"), g + 1)
                for j in range(2):
                    for s in range(RING):
                        pool.wait_ge(sem("slots_free"), g * BODY + (j * RING + s + 1))
                        pool.sem_inc(sem("slot_opened"), 1)
                        if s == 0:
                            pool.tensor_copy(idx_now[:, j * RING:(j + 1) * RING],
                                             idx[:, bass.ds(g * BODY + (j * RING - layer * NBLK * SLOTS), RING)]
                                             ).then_inc(sem("idx_staged"), 1)
                            pool.wait_ge(sem("idx_staged"), g * 2 + (j + 1))
                            pool.sem_inc(sem("slot_opened"), 1)
                        pool.indirect_dma_start(
                            ring[:, s], None, io[f"experts{layer}"],
                            bass.IndirectOffsetOnAxis(idx_now[:, j * RING + s:j * RING + s + 1], 0),
                        ).then_inc(sem(f"rows_in{s}"), 16)

            for layer in range(DEPTH):
                with pool.Fori(layer * NBLK * STEPS, (layer + 1) * NBLK * STEPS) as g:
                    gather_step(layer, g)

        @block.tensor
        def _(pe):
            lane = Lane(pe, "pe_own")
            jobs = {"act": 0, "dve": 0}
            chunks = [0]

            def fill(kind):
                n = jobs[kind]
                if n >= 3:
                    pe.wait_ge(sem(kind + "_emptied"), n - 2)
                jobs[kind] = n + 1
                return (act_banks if kind == "act" else dve_banks)[n % 3]

            def emptied(kind, number=None):
                pe.wait_ge(sem(kind + "_emptied"), number or jobs[kind])

            def next_chunk():
                n = chunks[0]
                chunks[0] += 1
                pe.wait_ge(sem(f"chunk_in{n % NWB}"), 16 * (n // NWB + 1))
                return wbuf[:, n % NWB]

            def chunk_used(kind):
                pe.wait_ge(sem(kind + "_full"), jobs[kind])
                pe.sem_inc(sem("chunks_free"), 1)

            def in_chunk(layer, c):
                if c >= KEEP:
                    return next_chunk()
                pe.wait_ge(sem("kept_in"), 16 * KEEP * (layer + 1))
                return kept[:, c]

            def in_chunk_used(kind, layer, b, c):
                if c >= KEEP:
                    chunk_used(kind)
                elif c == KEEP - 1 and b == NBLK - 1 and layer < DEPTH - 1:
                    pe.wait_ge(sem(kind + "_full"), jobs[kind])
                    pe.sem_inc(sem("kept_free"), 1)

            def row_products(out, lhsT, w, first=True, last=True, cols=CW, tick=None, halfway=None):
                for k in range(KD):
                    ins = pe.matmul(out[:, 0:cols], lhsT[:, k], w[:, k], start=first and k == 0,
                                    stop=last and k == KD - 1)
                    if tick is not None and k % 2 and k < KD - 1:
                        yield tick + k // 2 + 1
                    if halfway and k == KD // 2 - 1:
                        halfway()
                return ins

            def column_products(out, w, tick, tiles=range(CW // P)):
                for n, j in enumerate(tiles):
                    if n:
                        yield tick + n
                    for k in range(KD):
                        ins = pe.matmul(out[:, n * P:(n + 1) * P], w[:, k, j * P:(j + 1) * P], hnT[:, k],
                                        start=k == 0, stop=k == KD - 1)
                return ins

            def transposes(src, n, kind="act"):
                out = fill(kind)
                for j in range(n):
                    ins = pe.transpose(out[:, j * P:(j + 1) * P], src[:, j * P:(j + 1) * P], ident)
                ins.then_inc(sem(kind + "_full"), 1)

            def norm_transposes(b):
                lane.need("hn_ready")
                transposes(hn[:, b, 0:4 * P], 4)
                transposes(hn[:, b, 4 * P:8 * P], 4)

            def mixer0(b):
                yield 1
                norm_transposes(b)
                emptied("act")
                groups = head_groups(b)

                def score(heads):
                    keys = (b + 1) * P
                    out = fill("dve")
                    for j, hd in enumerate(heads):
                        off = hd % 2 * HD
                        ins = pe.matmul(out[:, j * keys:(j + 1) * keys], qT_att[off:off + HD, hd // 2],
                                        kT[off:off + HD, hd // 2, 0:keys], start=True, stop=True)
                    ins.then_inc(sem("dve_full"), 1)

                def first_scores():
                    emptied("act", qk_in)
                    score(groups[0])
                    score(groups[1])

                for c, kind in enumerate(("dve", "dve", "act", "act")):
                    yield T_IN0 + 4 * c
                    if c == 3:
                        lane.need("qk_ready")
                        for i in range(2):
                            transposes(qk[:, i], 4)
                        qk_in = jobs["act"]
                    w = in_chunk(0, c)
                    out = fill(kind)
                    ins = yield from row_products(out, hnT, w, tick=T_IN0 + 4 * c,
                                                  halfway=first_scores if c == 3 else None)
                    ins.then_inc(sem(kind + "_full"), 1)
                    in_chunk_used(kind, 0, b, c)
                yield T_IN0 + 16
                pe.wait_ge(sem("bands_loaded"), 16)
                pe.wait_ge(sem("pool_w_loaded"), 16)
                out = fill("act")
                for n in range(NWIN):
                    cols = slice(n * P, (n + 1) * P)
                    ins = pe.matmul(out[:, cols], pool_in[:, b, cols], bands[:, min(b, 1), n],
                                    start=True, stop=b == 0)
                    if b:
                        ins = pe.matmul(out[:, cols], pool_in[:, b - 1, cols], bands[:, 2, n],
                                        start=False, stop=True)
                ins.then_inc(sem("act_full"), 1)

                yield T_IN0 + 17
                emptied("act")
                out = fill("dve")
                for n in range(NWIN):
                    ins = pe.matmul(out[:, n * P:(n + 1) * P], pool_w[:, n], mixedT[:, n],
                                    start=True, stop=True)
                ins.then_inc(sem("dve_full"), 1)
                for i, heads in enumerate(groups):
                    yield T_ATT + 3 * i + 4
                    if i + 2 < len(groups):
                        score(groups[i + 2])
                    lane.need("probs_ready")
                    transposes(probs[:, i % 2], 4)
                    yield T_ATT + 3 * i + 5
                    emptied("act")
                    out = fill("act")
                    for j, hd in enumerate(heads):
                        off = hd % 2 * HD
                        for k in range(b + 1):
                            tile = j * (b + 1) + k
                            ins = pe.matmul(out[off:off + HD, j * P:(j + 1) * P],
                                            v_rows[:, k, hd * HD:(hd + 1) * HD],
                                            probsT[:, tile * P:(tile + 1) * P], start=k == 0, stop=k == b)
                    ins.then_inc(sem("act_full"), 1)
                for n in range(2):
                    yield T_OUT0 + 4 * n
                    if n == 0:
                        emptied("act")
                        emptied("dve")
                    w = next_chunk()
                    out = fill("dve")
                    ins = yield from row_products(out, mixT, w, tick=T_OUT0 + 4 * n)
                    ins.then_inc(sem("dve_full"), 1)
                    chunk_used("dve")

            def mixer1(b):
                yield 1
                norm_transposes(b)
                emptied("act")
                yield T_IN1 - 2
                pe.wait_ge(sem("dtw_loaded"), 16)
                out = fill("dve")
                ins = yield from row_products(out, hnT, dtw, cols=SH)
                ins.then_inc(sem("dve_full"), 1)
                for c in range(8):
                    at = T_IN1 + 4 * c
                    yield at
                    if c == 1:
                        lane.need("da_ready")
                        out = fill("dve")
                        pe.matmul(out[:, 0:SH], tri, dtv[:, 1], start=True, stop=True)
                        pe.matmul(out[:, SH:2 * SH], stri, dtv[:, 1], start=True, stop=True
                                  ).then_inc(sem("dve_full"), 1)
                    if c >= 2:
                        lane.need("conv_ready")
                        d = c - 2
                        transposes(xT[:, d % 2] if d < 4 else
                                   bcT[:, (d - 4) * 4:(d - 3) * 4].rearrange("p g t -> p (g t)"), 4)
                    w = in_chunk(1, c)
                    out = fill("act")
                    ins = yield from column_products(out, w, at)
                    ins.then_inc(sem("act_full"), 1)
                    in_chunk_used("act", 1, b, c)
                yield T_CB
                lane.need("bc_ready")
                for half in range(2):
                    out = fill("dve")
                    for j in range(4):
                        g = half * 4 + j
                        ins = pe.matmul(out[:, j * P:(j + 1) * P], bcT[:, g], bcT[:, SG + g], start=True, stop=True)
                    ins.then_inc(sem("dve_full"), 1)
                    yield T_CB + 1
                if b + 1 < NBLK:
                    lane.need("xdtw_ready")
                    for half in range(4):
                        yield T_CB + 2 + half
                        out = fill("act")
                        for j in range(2):
                            g = half * 2 + j
                            ins = pe.matmul(out[:, j * GW:(j + 1) * GW], b_rows[:, g * SN:(g + 1) * SN],
                                            y[:, g * GW:(g + 1) * GW], start=True, stop=True)
                        ins.then_inc(sem("act_full"), 1)
                    pe.wait_ge(sem("act_full"), jobs["act"])
                    pe.sem_inc(sem("xdtw_taken"), 1)

                def decays(g):
                    out = fill("dve")
                    for r in range(HPG):
                        head = g * HPG + r
                        ins = pe.matmul(out[:, r * P:(r + 1) * P], dtv[:, 1, head:head + 1].to_broadcast([P, P]),
                                        tri, start=True, stop=True)
                    ins.then_inc(sem("dve_full"), 1)

                def group_out(g):
                    lane.need("weights_ready")
                    out = fill("dve")
                    for r in range(HPG):
                        head = g * HPG + r
                        ins = pe.matmul(out[:, r * SP_:(r + 1) * SP_], decay[:, g % DBUF, r],
                                        xdt[:, head * SP_:(head + 1) * SP_], start=True, stop=True)
                    if b:
                        ins = pe.matmul(out[:, GW:2 * GW], bcT[:, SG + g], state[:, g], start=True, stop=True)
                    ins.then_inc(sem("dve_full"), 1)

                for g in range(SG + 1):
                    yield T_SCAN + 3 * g
                    if g < SG:
                        decays(g)
                        if g % 2 == 0:
                            w = next_chunk()
                            out_z = fill("act")
                    for part in range(2):
                        yield T_SCAN + 3 * g + 1 + part
                        if part == 0 and g:
                            group_out(g - 1)
                        if g < SG:
                            for k in range(4 * (g % 2) + 2 * part, 4 * (g % 2) + 2 * part + 2):
                                ins = pe.matmul(out_z, hnT[:, k], w[:, k], start=k == 0, stop=k == KD - 1)
                    if g < SG and g % 2:
                        ins.then_inc(sem("act_full"), 1)
                        chunk_used("act")
                yield T_YT
                lane.need("y_ready")
                for c in range(4):
                    transposes(y[:, c * CW:(c + 1) * CW], 4, "dve")
                yTk = yT.rearrange("p (half k) t -> p half k t", half=2)
                for n in range(2):
                    for half in range(2):
                        at = T_OUT1 + 4 * (2 * n + half)
                        yield at
                        if n == half == 0:
                            emptied("dve")
                        if half == 0:
                            out = fill("dve")
                        w = next_chunk()
                        ins = yield from row_products(out, yTk[:, half], w, half == 0, half == 1, tick=at)
                        if half:
                            ins.then_inc(sem("dve_full"), 1)
                            chunk_used("dve")
                        else:
                            lane(ins)
                            pe.sem_inc(sem("chunks_free"), 1)

            def queries(layer, b, base):
                yield base + 1
                norm_transposes(b)
                emptied("act")
                pe.sem_inc(sem("hn_transposed"), 1)

                for hd in range(PH):
                    at = base + T_Q + T_PART * hd
                    yield at
                    if hd % 2 == 0:
                        w = next_chunk()
                    out = fill("act")
                    ins = yield from column_products(out, w, at, range(2 * (hd % 2), 2 * (hd % 2) + 2))
                    ins.then_inc(sem("act_full"), 1)
                    if hd % 2:
                        chunk_used("act")
                    yield at + 2
                    pe.wait_ge(sem("keys_loaded"), 16)
                    emptied("act")
                    out = fill("act")
                    for i in range(2):
                        ins = pe.matmul(out[:, i * NK:(i + 1) * NK], qT[:, 2 * hd + i], keysT[:, layer, i],
                                        start=True, stop=True)
                    ins.then_inc(sem("act_full"), 1)

            def side(layer, b):
                yield from (mixer1 if layer else mixer0)(b)
                yield from queries(layer, b, T_END[layer])

            def sum_slot(g, n, start=False, stop=False):
                if n % GROUP == 0:
                    pe.wait_ge(sem("diag_ready"), g * GROUPS + (n // GROUP + 1))
                slot = n % RING
                for half in range(2):
                    ins = pe.matmul(acc[half], diag[:, n % DIAGS], ring[:, slot, D + half * CW:D + (half + 1) * CW],
                                    start=start, stop=stop, skip_group_check=True)
                ins.then_inc(sem("slots_free"), 1)

            def experts(phase, beside):
                first = phase * STEPS
                looped = first + UNROLLED[phase]
                total = UNROLLED[phase] * BODY
                for n in range(total + GROUP):
                    if n == GROUP and phase:
                        pe.wait_ge(sem("acc_read"), phase)
                    if n >= GROUP:
                        at = n - GROUP
                        sum_slot(first + at // BODY, at % BODY, start=at == 0, stop=at == SLOTS - 1)
                    if n < total:
                        beside.upto(pace(phase, n))
                if looped < first + STEPS:
                    with pe.Fori(looped, first + STEPS - 1) as g:
                        for n in range(BODY):
                            sum_slot(g, n)
                    for n in range(BODY):
                        sum_slot(first + STEPS - 1, n, stop=n == BODY - 1)

            pe.sem_inc(sem("chunks_free"), NWB)
            pe.sem_inc(sem("slots_free"), RING)
            pe.wait_ge(sem("consts_loaded"), 16)
            beside = Side(one_after_another(side))
            beside.upto(T_END0 + T_FIRST - 1)
            for phase in range(PHASES):
                experts(phase, beside)

        @block.scalar
        def _(act):
            lane = Lane(act, "act_own")
            banks_in = Emptier(act, "act", act_banks)

            def f(out, in_, func, name=None, **more):
                lane(act.activation(out, in_, func, **more), name)

            def empty(out, func=ACT.Copy, pattern=None, cols=CW, **dims):
                src = banks_in.take()[:, 0:cols]
                f(out, src.rearrange(pattern, **dims) if pattern else src, func, "act_emptied")

            def norm(base):
                yield base + 1
                for n in range(2):
                    empty(hnT[:, 4 * n:4 * n + 4], pattern="p (k t) -> p k t", k=4)

            def mixer0(b):
                yield from norm(0)
                yield T_IN0 + 12
                empty(pool_in[:, b])
                empty(qT_att, pattern="p (n t) -> p n t", n=4)
                empty(kT[:, :, b * P:(b + 1) * P], pattern="p (n t) -> p n t", n=4)

                def exp_scores(i):
                    lane.need("scores_biased")
                    f(probs[:, i % 2], probs[:, i % 2], ACT.Exp)
                    lane.tell("scores_exp")

                groups = head_groups(b)
                yield T_ATT + 1
                exp_scores(0)
                yield T_IN0 + 16
                empty(v_rows[:, b])
                empty(mixedT, pattern="p (n c) -> p n c", n=NWIN)
                for i, heads in enumerate(groups):
                    if i + 1 < len(groups):
                        yield T_ATT + 3 * i + 3
                        exp_scores(i + 1)
                    yield T_ATT + 3 * i + 4
                    empty(probsT)
                    lane.tell("probs_taken")
                    yield T_ATT + 3 * i + 6
                    off, n = heads[0] % 2 * HD, len(heads)
                    first = NWIN + heads[0] // 2
                    src = banks_in.take()[off:off + HD, 0:n * P].rearrange("p (k t) -> p k t", k=n)
                    f(mixT[off:off + HD, first:first + n], src, ACT.Copy, "act_emptied")

            def mixer1(b):
                yield from norm(0)
                yield T_IN1 - 1
                lane.need("dt_abs")
                f(dtv[:, 6], dtv[:, 2], ACT.Exp, scale=-1.0)
                f(dtv[:, 6], dtv[:, 6], ACT.Ln, bias=1.0)
                lane.tell("dt_log")

                def silu(d):
                    act.wait_ge(sem("conv_done"), 8 * b + d + 1)
                    if d < 4:
                        f(xT[:, d % 2], xT[:, d % 2], ACT.Silu)
                    else:
                        f(bcT[:, (d - 4) * 4:(d - 3) * 4].rearrange("p g t -> p (g t)"), xT[:, d % 2], ACT.Silu)
                    lane.tell("conv_ready" if d < 6 else "c_ready")

                for c in range(8):
                    yield T_IN1 + 4 * c + 4
                    empty(conv_in[:, c % 2, :, TAPS - 1:], pattern="p (j t) -> p j t", j=4)
                    lane.tell("conv_loaded")
                    if 1 <= c < 7:
                        d = c - 1
                        empty(x_rows[:, d * CW:(d + 1) * CW] if d < 4 else b_rows[:, (d - 4) * CW:(d - 3) * CW])
                        lane.tell("conv_rows")
                    yield T_IN1 + 4 * c + 7
                    silu(c)
                    if c == 1:
                        lane.need("sums_ready")
                        f(dtv[:, 5:7].rearrange("p n c -> p (n c)"), dtv[:, 3:5].rearrange("p n c -> p (n c)"), ACT.Exp)
                        lane.tell("decay_factors")
                lane.tell("bc_ready")
                if b + 1 < NBLK:
                    for half in range(4):
                        yield T_CB + 2 + half
                        empty(state[:, 2 * half:2 * half + 2], pattern="p (g c) -> p g c", g=2)
                for g in range(SG):
                    yield T_SCAN + 3 * g + 2
                    lane.need("decay_args")
                    f(decay[:, g % DBUF], decay[:, g % DBUF], ACT.Exp)
                    lane.tell("decay_exp")
                    if g % 2:
                        c = g // 2
                        yield T_SCAN + 3 * g + 3
                        if c >= 2:
                            act.wait_ge(sem("z_used"), 4 * b + c - 1)
                        empty(xT[:, c % 2], ACT.Silu)
                        lane.tell("z_ready")

            def queries(layer, b, base):
                yield base
                yield from norm(base)
                if layer == 0 and b == NBLK - 1:
                    for which in range(2):
                        act.dma_start(gains[:, which], gain_rows(1, which)).then_inc(sem(f"gain_loaded{which}"), 16)

                for hd in range(PH):
                    at = base + T_Q + T_PART * hd
                    yield at + 2
                    empty(qT[:, 2 * hd:2 * hd + 2], pattern="p (m t) -> p m t", cols=2 * P, m=2)
                    yield at + 3
                    if hd == 0:
                        lane.need("root_ready")
                    f(scores[:, 2 * hd:2 * hd + 2], banks_in.take()[:, 0:2 * NK].rearrange("p (m k) -> p m k", m=2),
                      ACT.Copy, "act_emptied", scale=norm_root)
                    lane.tell("scores_ready")
                    yield base + T_TOP + T_PART * hd + 2
                    lane.need("best_ready")
                    f(expd, expd, ACT.Exp)
                    lane.tell("best_exp")

            def side(layer, b):
                yield from (mixer1 if layer else mixer0)(b)
                yield from queries(layer, b, T_END[layer])

            def take_gelu(g, q):
                cols = slice(q * GROUP, (q + 1) * GROUP)
                act.wait_ge(sem("dot_done"), g * BODY + (q + 1) * GROUP)
                act.activation(acts[:, cols], dots[:, cols], ACT.Gelu).then_inc(sem("gelu_done"), 1)

            def make_diagonals(g, q):
                act.wait_ge(sem("coef_done"), g * GROUPS + (q + 1))
                act.wait_ge(sem("slots_free"), g * BODY + ((q + 1) * GROUP + RING - DIAGS))
                for s in range(GROUP):
                    ins = act.activation(diag[:, (q * GROUP + s) % DIAGS], ident, ACT.Copy,
                                         scale=coefs[:, q * GROUP + s:q * GROUP + s + 1])
                ins.then_inc(sem("diag_ready"), 1)

            def experts(phase, beside):
                first = phase * STEPS
                looped = first + UNROLLED[phase]
                for n in range(UNROLLED[phase] * BODY):
                    g, q = first + n // BODY, n % BODY // GROUP
                    if n % GROUP == GROUP - 1:
                        take_gelu(g, q)
                    beside.upto(pace(phase, n))
                    if n % GROUP == GROUP - 1:
                        make_diagonals(g, q)
                if looped < first + STEPS:
                    with act.Fori(looped, first + STEPS) as g:
                        for q in range(GROUPS):
                            take_gelu(g, q)
                            make_diagonals(g, q)

            act.wait_ge(sem("consts_loaded"), 16)
            act.wait_ge(sem("rows_loaded"), 16)
            f(eA, a_log, ACT.Exp)
            beside = Side(one_after_another(side))
            beside.upto(T_END0 + T_FIRST - 1)
            for phase in range(PHASES):
                experts(phase, beside)

        @block.vector
        def _(dve):
            lane = Lane(dve, "dve_own")
            banks_in = Emptier(dve, "dve", dve_banks)

            def tt(out, in0, in1, op=ALU.mult, name=None):
                lane(dve.tensor_tensor(out, in0, in1, op), name)

            def ts(out, in0, s1, s2, op0, op1=None, name=None):
                more = () if op1 is None else (op1,)
                lane(dve.tensor_scalar(out, in0, s1, s2, op0, *more), name)

            def stt(out, in0, scalar, in1, op0, op1, name=None):
                lane(dve.scalar_tensor_tensor(out, in0, scalar, in1, op0, op1), name)

            def add_to_stream(b, n, src, name):
                part = h[:, b, n * CW:(n + 1) * CW]
                tt(part, part, src, ALU.add, name)

            def inverse_root(n):
                v, r, t = stat[:, 0:n], stat[:, 32:32 + n], stat[:, 48:48 + n]
                ts(t.bitcast(u32), v.bitcast(u32), 1, None, ALU.logical_shift_right)
                ts(r.bitcast(u32), t.bitcast(u32), -1.0, float(0x5F3759DF), ALU.mult, ALU.add)
                for _ in range(3):
                    stt(t, r, -0.5, r, ALU.mult, ALU.mult)
                    tt(t, t, v)
                    stt(r, t, 1.5, r, ALU.add, ALU.mult)

            def mean_square(b, out):
                lane(dve.tensor_tensor_reduce(out=out, in0=h[:, b], in1=h[:, b], scale=1.0, scalar=0.0,
                                              op0=ALU.mult, op1=ALU.add, accum_out=stat[:, 0:1]))
                ts(stat[:, 0:1], stat[:, 0:1], 1.0 / D, EPS, ALU.mult, ALU.add)
                inverse_root(1)

            def norm(layer, b):
                dve.wait_ge(sem(f"x_loaded{b}"), 16)
                mean_square(b, hn[:, b])
                dve.wait_ge(sem("gain_loaded0"), 16 * (layer + 1))
                stt(hn[:, b], h[:, b], stat[:, 32:33], gains[:, 0], ALU.mult, ALU.mult)
                lane.tell("hn_ready")

            def mixer0(b):
                norm(0, b)
                for i in range(2):
                    yield T_IN0 + 4 + 4 * i
                    lane(dve.tensor_copy(qk[:, i], banks_in.take()), "dve_emptied")
                flat = qk.rearrange("p i c -> p (i c)")
                heads = flat.rearrange("p (m e) -> p m e", e=HD)
                tt(qk_sq, flat, flat)
                yield T_IN0 + 9
                lane(dve.reduce_sum(stat[:, 0:16], qk_sq.rearrange("p (m e) -> p m e", e=HD), AX))
                ts(stat[:, 0:16], stat[:, 0:16], 1.0 / HD, EPS, ALU.mult, ALU.add)
                inverse_root(2 * HEADS)
                yield T_IN0 + 10
                tt(heads, heads, stat[:, 32:48].unsqueeze(2).to_broadcast([P, 2 * HEADS, HD]))
                yield T_IN0 + 11
                dve.wait_ge(sem("rows_loaded"), 16)
                for i in range(2):
                    part = qk[:, i].rearrange("p (m e) -> p m e", e=HD)
                    tt(part, part, qk_gain[:, i:i + 1].to_broadcast([P, HEADS, HD]))
                lane.tell("qk_ready")
                dve.wait_ge(sem("bias_loaded"), 16)
                keys = (b + 1) * P
                groups = head_groups(b)

                def pool_out():
                    dve.wait_ge(sem("cols_loaded"), 16)
                    tt(mixT[:, 0:NWIN], banks_in.take().rearrange("p (n t) -> p n t", n=NWIN),
                       pool_scale.unsqueeze(2).to_broadcast([P, NWIN, P]), name="dve_emptied")

                def bias_scores(i):
                    if i >= 2:
                        lane.need("probs_taken")
                    out = banks_in.take()
                    for j, hd in enumerate(groups[i]):
                        cols = slice(j * keys, (j + 1) * keys)
                        stt(probs[:, i % 2, cols], out[:, cols], HD ** -0.5, bias_t[:, hd, 2 * P - keys:],
                            ALU.mult, ALU.add, "dve_emptied" if hd == groups[i][-1] else None)
                    part = probs[:, i % 2].rearrange("p (j k) -> p j k", k=keys)
                    n = len(groups[i])
                    top = stat[:, 64:64 + n]
                    lane(dve.reduce_max(top, part, AX))
                    tt(part, part, top.unsqueeze(2).to_broadcast([P, n, keys]), ALU.subtract)
                    lane.tell("scores_biased")

                yield T_ATT
                bias_scores(0)
                for i, group in enumerate(groups):
                    if i + 1 < len(groups):
                        yield T_ATT + 3 * i + 2
                        if i == 1:
                            pool_out()
                        bias_scores(i + 1)
                    elif i == 1:
                        pool_out()
                    yield T_ATT + 3 * i + 3
                    lane.need("scores_exp")
                    n = len(group)
                    total = stat[:, 68:68 + n]
                    part = probs[:, i % 2].rearrange("p (j k) -> p j k", k=keys)
                    lane(dve.reduce_sum(total, part, AX))
                    lane(dve.reciprocal(total, total))
                    tt(part, part, total.unsqueeze(2).to_broadcast([P, n, keys]))
                    lane.tell("probs_ready")
                yield T_ATT + 14
                for n in range(2):
                    lane.need("probs_taken")
                for n in range(2):
                    yield T_OUT0 + 4 * n + 4
                    add_to_stream(b, n, banks_in.take(), "dve_emptied")

            def mixer1(b):
                norm(1, b)
                yield T_IN1 - 1
                tt(dtv[:, 0], banks_in.take()[:, 0:SH], dt_bias, ALU.add, "dve_emptied")
                stt(dtv[:, 2], dtv[:, 0], -1.0, dtv[:, 0], ALU.mult, ALU.max)
                lane.tell("dt_abs")
                yield T_IN1
                lane.need("dt_log")
                stt(dtv[:, 0], dtv[:, 0], 0.0, dtv[:, 6], ALU.max, ALU.add)
                stt(dtv[:, 1], dtv[:, 0], -1.0, eA, ALU.mult, ALU.mult)
                lane.tell("da_ready")
                for c in range(8):
                    yield T_IN1 + 4 * c + 5
                    if c >= 2:
                        lane.need("conv_rows")
                    lane.need("conv_loaded")
                    tiles = conv_in[:, c % 2]
                    tails = carry[:, 4 * c:4 * c + 4]
                    if b:
                        lane(dve.tensor_copy(tiles[:, :, 0:TAPS - 1], tails))
                    else:
                        lane(dve.memset(tiles[:, :, 0:TAPS - 1], 0.0))
                        lane(dve.tensor_copy(tails, tiles[:, :, P:]))
                    if c == 1:
                        lane(dve.tensor_copy(dtv[:, 3:5].rearrange("p n c -> p (n c)"), banks_in.take()[:, 0:2 * SH]),
                             "dve_emptied")
                        lane.tell("sums_ready")
                    for pair in range(2):
                        for tap in range(TAPS):
                            for j in (2 * pair, 2 * pair + 1):
                                t = 4 * c + j
                                out = xT[:, c % 2, j * P:(j + 1) * P]
                                if tap == 0:
                                    done = lane.start(dve.tensor_scalar(
                                        out, tiles[:, j, 0:P], taps[:, t, 0:1], conv_b[:, t:t + 1], ALU.mult, ALU.add))
                                else:
                                    lane.after((done[0], done[1] - 1))
                                    done = lane.start(dve.scalar_tensor_tensor(
                                        out, tiles[:, j, tap:tap + P], taps[:, t, tap:tap + 1], out,
                                        ALU.mult, ALU.add))
                        lane.after(done)
                        if pair == 0:
                            yield T_IN1 + 4 * c + 6
                    lane.tell("conv_done")
                by_head = "p (h e) -> p h e"
                step = dtv[:, 0].unsqueeze(2).to_broadcast([P, SH, SP_])
                yield T_CB - 2
                tt(xdt.rearrange(by_head, h=SH), x_rows.rearrange(by_head, h=SH), step)
                yield T_CB - 1
                lane.need("decay_factors")
                if b + 1 < NBLK:
                    tt(y.rearrange(by_head, h=SH), xdt.rearrange(by_head, h=SH),
                       dtv[:, 6].unsqueeze(2).to_broadcast([P, SH, SP_]))
                    lane.tell("xdtw_ready")
                for half in range(2):
                    yield T_CB + 1 + half
                    tt(cb[:, 4 * half:4 * half + 4], banks_in.take().rearrange("p (g l) -> p g l", g=4),
                       tri.unsqueeze(1).to_broadcast([P, 4, P]), name="dve_emptied")
                yield T_CB + 5
                if b + 1 < NBLK:
                    lane.need("xdtw_taken")
                tt(y.rearrange(by_head, h=SH), x_rows.rearrange(by_head, h=SH),
                   d_skip.unsqueeze(2).to_broadcast([P, SH, SP_]))

                def decay_args(g):
                    out = banks_in.take()
                    for r in range(HPG):
                        head = g * HPG + r
                        done = lane.start(dve.tensor_scalar(
                            decay[:, g % DBUF, r], out[:, r * P:(r + 1) * P], dtv[:, 3, head:head + 1], 0.0,
                            ALU.subtract, ALU.min), "dve_emptied" if r == HPG - 1 else None)
                    lane.after(done)
                    lane.tell("decay_args")

                def group_out(g):
                    out = banks_in.take()
                    part = y[:, g * GW:(g + 1) * GW]
                    if b:
                        tt(y_tmp.rearrange(by_head, h=HPG), out[:, GW:2 * GW].rearrange(by_head, h=HPG),
                           dtv[:, 5, g * HPG:(g + 1) * HPG].unsqueeze(2).to_broadcast([P, HPG, SP_]))
                        tt(part, part, y_tmp, ALU.add)
                    tt(part, part, out[:, 0:GW], ALU.add, "dve_emptied")

                def gate_and_square(c):
                    lane.need("z_ready")
                    part, square = y[:, c * CW:(c + 1) * CW], x_rows[:, c * CW:(c + 1) * CW]
                    tt(part, part, xT[:, c % 2])
                    lane.tell("z_used")
                    tt(square, part, part)
                    lane(dve.reduce_sum(stat[:, 2 * c:2 * c + 2], square.rearrange("p (g c) -> p g c", g=2), AX))

                for g in range(SG + 1):
                    if g < SG:
                        yield T_SCAN + 3 * g + 1
                        decay_args(g)
                    if g:
                        yield T_SCAN + 3 * g + 2
                        group_out(g - 1)
                    yield T_SCAN + 3 * g + 3
                    if g < SG:
                        lane.need("decay_exp")
                        tt(decay[:, g % DBUF], decay[:, g % DBUF], cb[:, g:g + 1].to_broadcast([P, HPG, P]))
                        lane.tell("weights_ready")
                    if g and g % 2 == 0:
                        gate_and_square(g // 2 - 1)
                yield T_SCAN + 28
                ts(stat[:, 0:SG], stat[:, 0:SG], 1.0 / GW, EPS, ALU.mult, ALU.add)
                inverse_root(SG)
                grouped = y.rearrange("p (g c) -> p g c", g=SG)
                for half in range(2):
                    yield T_SCAN + 28 + half
                    part = slice(half * SG // 2, (half + 1) * SG // 2)
                    scale = stat[:, 32:32 + SG][:, part]
                    tt(grouped[:, part], grouped[:, part], scale.unsqueeze(2).to_broadcast([P, SG // 2, GW]))
                lane.tell("y_ready")
                for c in range(4):
                    yield T_YT + 1 + c // 2
                    tt(yT[:, 4 * c:4 * c + 4], banks_in.take().rearrange("p (k t) -> p k t", k=4),
                       gate_gain[:, 4 * c:4 * c + 4].unsqueeze(2).to_broadcast([P, 4, P]), name="dve_emptied")
                for n in range(2):
                    yield T_OUT1 + 8 * n + 8
                    add_to_stream(b, n, banks_in.take(), "dve_emptied")

            def top16(*rows):
                steps = [
                    lambda src, values, places: dve.max(values[:, 0:8], src),
                    lambda src, values, places: dve.max_index(places[:, 0:8], values[:, 0:8], src),
                    lambda src, values, places: dve.match_replace(src, values[:, 0:8], src, NEG),
                    lambda src, values, places: dve.max(values[:, 8:16], src),
                    lambda src, values, places: dve.max_index(places[:, 8:16], values[:, 8:16], src),
                ]
                started = [None] * len(rows)
                for step in steps:
                    for n, row in enumerate(rows):
                        if started[n]:
                            lane.after(started[n])
                        started[n] = lane.start(step(*row))
                lane.after(started[-1])

            def routing(layer, b, base):
                yield base
                dve.wait_ge(sem("gain_loaded1"), 16 * (layer + 1))
                tt(hn[:, b], h[:, b], gains[:, 1])
                lane.tell("hn_ready")
                mean_square(b, squares)
                lane(dve.tensor_copy(norm_root, stat[:, 32:33]))
                yield base + 2
                lane.need("hn_transposed")
                ts(hn[:, b], hn[:, b], norm_root, None, ALU.mult)
                lane.tell("root_ready")
                dve.wait_ge(sem("consts_loaded"), 16)

                def candidates(hd):
                    first, second = top_s[:, 0:TOPK], top_s[:, TOPK:]
                    grid = cand[:, 0:WHOLE * TOPK].rearrange("p (a b) -> p a b", a=WHOLE)
                    lane.start(dve.tensor_tensor(grid, first[:, 0:WHOLE].unsqueeze(2).to_broadcast([P, WHOLE, TOPK]),
                                                 second.unsqueeze(1).to_broadcast([P, WHOLE, TOPK]), ALU.add))
                    ts(cand[:, WHOLE * TOPK:], first[:, WHOLE:], second[:, 0:1], None, ALU.add)
                    top16((cand, best, best_pos))

                def expert_numbers(hd):
                    row, place, beyond = (pos_f[:, n * TOPK:(n + 1) * TOPK] for n in range(3))
                    key = top_if.rearrange("p (i a) -> p i a", i=2)
                    started = [lane.start(dve.tensor_scalar(pos_hi, best_pos, 4, None, ALU.logical_shift_right)),
                               lane.start(dve.tensor_scalar(pos_lo, best_pos, 15, None, ALU.bitwise_and)),
                               lane.start(dve.tensor_copy(top_if, top_i))]
                    lane.after(started[0])
                    lane.start(dve.tensor_copy(row, pos_hi))
                    lane.after(started[1])
                    lane(dve.tensor_copy(place, pos_lo))
                    stt(beyond, row, float(WHOLE), place, ALU.is_ge, ALU.mult)
                    lane.start(dve.tensor_tensor(row, row, beyond, ALU.add))
                    tt(place, place, beyond, ALU.subtract)
                    hot = onehot.rearrange("p (i s a) -> p i s a", i=2, s=TOPK)
                    flat = onehot.rearrange("p (n a) -> p n a", a=TOPK)
                    tt(flat, pos_f[:, 0:2 * TOPK].unsqueeze(2).to_broadcast([P, 2 * TOPK, TOPK]),
                       iota16.unsqueeze(1).to_broadcast([P, 2 * TOPK, TOPK]), ALU.is_equal)
                    tt(hot, hot, key.unsqueeze(2).to_broadcast([P, 2, TOPK, TOPK]))
                    lane(dve.reduce_sum(picked, flat, AX))
                    stt(row, picked[:, 0:TOPK], float(NK), picked[:, TOPK:], ALU.mult, ALU.add)
                    at = b * SLOTS + hd * TOPK
                    lane(dve.tensor_copy(idx[:, at:at + TOPK], row))
                    lane.tell("idx_ready")

                for hd in range(PH):
                    at = base + T_TOP + T_PART * hd
                    yield at
                    lane.need("scores_ready")
                    top16(*((scores[:, 2 * hd + i], top_s[:, i * TOPK:(i + 1) * TOPK],
                             top_i[:, i * TOPK:(i + 1) * TOPK]) for i in range(2)))
                    yield at + 1
                    candidates(hd)
                    ts(expd, best, best[:, 0:1], None, ALU.subtract)
                    lane.tell("best_ready")
                    yield at + 2
                    expert_numbers(hd)
                    yield at + 3
                    lane.need("best_exp")
                    total = stat[:, 72:73]
                    lane(dve.reduce_sum(total, expd, AX))
                    lane(dve.reciprocal(total, total))
                    ts(gate[:, b * SLOTS + hd * TOPK:b * SLOTS + (hd + 1) * TOPK], expd, total, None, ALU.mult)

            def side(layer, b):
                yield from (mixer1 if layer else mixer0)(b)
                yield from routing(layer, b, T_END[layer])

            def dot(phase, g, n):
                slot = n % RING
                dve.wait_ge(sem(f"rows_in{slot}"), g * 32 + 16 * (n // RING + 1))
                dve.tensor_tensor_reduce(out=ring[:, slot, 0:D], in0=ring[:, slot, 0:D], in1=hn[:, phase % NBLK],
                                         scale=1.0, scalar=0.0, op0=ALU.mult, op1=ALU.add,
                                         accum_out=dots[:, n:n + 1]).then_inc(sem("dot_done"), 1)

            def coefficients(phase, g, q):
                dve.wait_ge(sem("gelu_done"), g * GROUPS + (q + 1))
                cols = slice(q * GROUP, (q + 1) * GROUP)
                at = g * BODY + (q * GROUP - phase // NBLK * NBLK * SLOTS)
                dve.tensor_tensor(coefs[:, cols], acts[:, cols], gate[:, bass.ds(at, GROUP)],
                                  ALU.mult).then_inc(sem("coef_done"), 1)

            def experts(phase, beside):
                first = phase * STEPS
                looped = first + UNROLLED[phase]
                for n in range(UNROLLED[phase] * BODY):
                    g = first + n // BODY
                    dot(phase, g, n % BODY)
                    beside.upto(pace(phase, n))
                    if n % GROUP == GROUP - 1:
                        coefficients(phase, g, n % BODY // GROUP)
                if looped < first + STEPS:
                    with dve.Fori(looped, first + STEPS) as g:
                        for n in range(BODY):
                            dot(phase, g, n)
                            if n % GROUP == GROUP - 1:
                                coefficients(phase, g, n // GROUP)
                dve.wait_ge(sem("slots_free"), (phase + 1) * SLOTS + RING)
                for n in range(2):
                    add_to_stream(phase % NBLK, n, acc[n], None)
                lane.tell("acc_read")
                if phase // NBLK == DEPTH - 1:
                    lane.tell("out_ready")

            dve.wait_ge(sem("x_loaded0"), 16)
            beside = Side(one_after_another(side))
            beside.upto(T_END0 + T_FIRST - 1)
            for phase in range(PHASES):
                experts(phase, beside)


def chunked(w):
    k, n = w.shape
    w = w.reshape(k // D, KD, P, n // CW, CW)
    return w.transpose(3, 0, 2, 1, 4).reshape(-1, P, CH)


def tiles_last(v):
    return v.reshape(-1, P).T


def kernel(**inputs):
    import concourse.bacc as bacc
    from concourse.bass_utils import run_bass_kernel_spmd

    a = {k: np.asarray(v) for k, v in inputs.items()}
    w_in = a["ssm_w_in"][0]
    even = a["even_w_in"][0]
    pooled, q_and_k, v = np.split(even, [POOL_W, POOL_W + 2 * AW], axis=1)
    consts, bands = shape_constants()
    weights = [chunked(np.concatenate([q_and_k, pooled, v], axis=1)), chunked(a["even_w_out"][0]), chunked(a["peer_w_q"][0]),
               chunked(w_in[:, SI:SI + XBC]), chunked(w_in[:, 0:SI]), chunked(a["ssm_w_out"][0]),
               chunked(a["peer_w_q"][1])]
    conv_w = a["conv_w"][0].reshape(TAPS, XT, P).transpose(2, 1, 0).reshape(P, XT * TAPS)
    arrays = {
        "x": a["x"].reshape(SEQ, D),
        "gains": np.stack([a["attn_norm"], a["ffn_norm"]], axis=1),
        "weights": np.concatenate(weights, axis=0),
        "dt_w": w_in[:, SI + XBC:],
        "rows": np.concatenate([a["q_gain"][0], a["k_gain"][0], a["dt_bias"][0], a["a_log"][0],
                                a["d_skip"][0]])[None, :],
        "cols": np.concatenate([tiles_last(a["pool_scale"][0]), conv_w, tiles_last(a["conv_b"][0]),
                                tiles_last(a["gate_gain"][0])], axis=1),
        "pool_w": a["pool_w"][0],
        "keysT": a["peer_sub_keys"].transpose(0, 1, 3, 2),
        "experts0": np.concatenate([a["peer_u"][0], a["peer_v"][0]], axis=1),
        "experts1": np.concatenate([a["peer_u"][1], a["peer_v"][1]], axis=1),
        "consts": consts, "bands": bands, "bias": attention_bias(),
    }
    arrays = {"in_" + k: np.ascontiguousarray(v) for k, v in arrays.items()}
    nc = bacc.Bacc("TRN2", target_bir_lowering=False, num_devices=1)
    io = {k[3:]: nc.dram_tensor(k, v.shape, mybir.dt.from_np(v.dtype), kind="ExternalInput").ap()
          for k, v in arrays.items()}
    io["out"] = nc.dram_tensor("out", (SEQ, D), mybir.dt.float32, kind="ExternalOutput").ap()
    build_trunk(nc, io)
    r = run_bass_kernel_spmd(nc, [arrays], core_ids=[0])
    return r.results[0]["out"].reshape(1, SEQ, D)
```
